# Optimizing a Trainium2 kernel written in Bass

```python
import math
import jax, jax.numpy as jnp
from jax import lax
import numpy as np

D_MODEL = 1024
BATCH = 1
SEQ = 512
DEPTH = 2

HEAD_DIM = 64
N_DIFF = 4
DIFF_V = 2 * HEAD_DIM
N_FOX = 8
N_SB = 8
N_BRANCH = 3
D_FF = 2816
Q_BLOCK = 128
EPS = 1e-6
SUBLN_EPS = 1e-5

A_QK = N_DIFF * 2 * HEAD_DIM
W_A = N_DIFF * DIFF_V
W_B = N_FOX * HEAD_DIM
W_C = N_SB * HEAD_DIM
IN_SIZES = (A_QK, A_QK, W_A, W_B, W_B, W_B, N_FOX, W_C, W_C, W_C, N_BRANCH * D_MODEL)
N_IN = 9 * 512 + N_FOX + N_BRANCH * D_MODEL

kernel_name = "hybrid_diff_fox_stickbreak_macaron"

def _rmsnorm(x, g, eps=EPS):
    x32 = x.astype(jnp.float32)
    y = x32 * lax.rsqrt(jnp.mean(x32 * x32, axis=-1, keepdims=True) + eps)
    return (y * g.astype(jnp.float32)).astype(x.dtype)

def _swiglu(x, w1, w3, w2):
    return (jax.nn.silu(x @ w1) * (x @ w3)) @ w2

def _alibi_slopes(n_heads):
    return jnp.asarray([2.0 ** (-8.0 * (h + 1) / n_heads) for h in range(n_heads)], jnp.float32)

def _sweep(block_fn, seq):
    out = lax.map(block_fn, jnp.arange(seq // Q_BLOCK))
    nb, b, h, qb, e = out.shape
    return out.transpose(1, 0, 3, 2, 4).reshape(b, nb * qb, h * e)

def _diff_attention(q, k, v, lq1, lk1, lq2, lk2, subln_g, lam_init):
    b, s = q.shape[:2]
    q = q.reshape(b, s, N_DIFF, 2, HEAD_DIM)
    k = k.reshape(b, s, N_DIFF, 2, HEAD_DIM)
    v = v.reshape(b, s, N_DIFF, DIFF_V)
    f32 = jnp.float32
    lam = (jnp.exp(jnp.sum(lq1.astype(f32) * lk1.astype(f32)))
           - jnp.exp(jnp.sum(lq2.astype(f32) * lk2.astype(f32))) + lam_init)
    slopes = _alibi_slopes(N_DIFF)[:, None, None, None]
    scale = 1.0 / math.sqrt(HEAD_DIM)
    key_pos = jnp.arange(s)

    def block(i):
        qb = lax.dynamic_slice_in_dim(q, i * Q_BLOCK, Q_BLOCK, axis=1)
        dist = (i * Q_BLOCK + jnp.arange(Q_BLOCK))[:, None] - key_pos[None, :]
        logits = (jnp.einsum('bqhcd,bkhcd->bhcqk', qb, k).astype(f32) * scale
                  - slopes * dist.astype(f32))
        logits = jnp.where(dist >= 0, logits, -jnp.inf)
        p = jax.nn.softmax(logits, axis=-1)
        attn = p[:, :, 0] - lam * p[:, :, 1]
        return jnp.einsum('bhqk,bkhe->bhqe', attn.astype(v.dtype), v)

    o = _sweep(block, s).reshape(b, s, N_DIFF, DIFF_V)
    o = _rmsnorm(o, subln_g, SUBLN_EPS) * (1.0 - lam_init)
    return o.reshape(b, s, W_A)

def _forgetting_attention(q, k, v, f_logit, f_bias):
    b, s = q.shape[:2]
    q = q.reshape(b, s, N_FOX, HEAD_DIM)
    k = k.reshape(b, s, N_FOX, HEAD_DIM)
    v = v.reshape(b, s, N_FOX, HEAD_DIM)
    f32 = jnp.float32
    log_f = jax.nn.log_sigmoid(f_logit.astype(f32) + f_bias.astype(f32))
    c = jnp.cumsum(log_f, axis=1).transpose(0, 2, 1)
    scale = 1.0 / math.sqrt(HEAD_DIM)
    key_pos = jnp.arange(s)

    def block(i):
        qb = lax.dynamic_slice_in_dim(q, i * Q_BLOCK, Q_BLOCK, axis=1)
        cq = lax.dynamic_slice_in_dim(c, i * Q_BLOCK, Q_BLOCK, axis=2)
        dist = (i * Q_BLOCK + jnp.arange(Q_BLOCK))[:, None] - key_pos[None, :]
        logits = (jnp.einsum('bqhd,bkhd->bhqk', qb, k).astype(f32) * scale
                  + cq[..., :, None] - c[..., None, :])
        logits = jnp.where(dist >= 0, logits, -jnp.inf)
        p = jax.nn.softmax(logits, axis=-1)
        return jnp.einsum('bhqk,bkhe->bhqe', p.astype(v.dtype), v)

    return _sweep(block, s)

def _stick_breaking_attention(q, k, v):
    b, s = q.shape[:2]
    q = q.reshape(b, s, N_SB, HEAD_DIM)
    k = k.reshape(b, s, N_SB, HEAD_DIM)
    v = v.reshape(b, s, N_SB, HEAD_DIM)
    f32 = jnp.float32
    scale = 1.0 / math.sqrt(HEAD_DIM)
    key_pos = jnp.arange(s)

    def block(i):
        qb = lax.dynamic_slice_in_dim(q, i * Q_BLOCK, Q_BLOCK, axis=1)
        dist = (i * Q_BLOCK + jnp.arange(Q_BLOCK))[:, None] - key_pos[None, :]
        strict = dist > 0
        z = jnp.einsum('bqhd,bkhd->bhqk', qb, k).astype(f32) * scale
        log_keep = jnp.where(strict, jax.nn.log_sigmoid(-z), 0.0)
        later = lax.cumsum(log_keep, axis=3, reverse=True) - log_keep
        w = jnp.where(strict, jnp.exp(jax.nn.log_sigmoid(z) + later), 0.0)
        return jnp.einsum('bhqk,bkhe->bhqe', w.astype(v.dtype), v)

    return _sweep(block, s)

def setup_inputs(seed: int = 0) -> dict:
    key = jax.random.key(seed)
    ks = jax.random.split(key, 24)
    f32 = jnp.float32

    def nrm(k, shape, fan_in):
        return jax.random.normal(k, shape, f32) * fan_in ** -0.5

    def gain(k, shape):
        return 1.0 + 0.05 * jax.random.normal(k, shape, f32)

    return {
        "x": jax.random.normal(ks[0], (BATCH, SEQ, D_MODEL), f32),
        "ffn1_norm": gain(ks[1], (DEPTH, D_MODEL)),
        "ffn1_w1": nrm(ks[2], (DEPTH, D_MODEL, D_FF), D_MODEL),
        "ffn1_w3": nrm(ks[3], (DEPTH, D_MODEL, D_FF), D_MODEL),
        "ffn1_w2": nrm(ks[4], (DEPTH, D_FF, D_MODEL), D_FF),
        "mix_norm": gain(ks[5], (DEPTH, D_MODEL)),
        "w_in": nrm(ks[6], (DEPTH, D_MODEL, N_IN), D_MODEL),
        "forget_bias": jax.random.uniform(ks[7], (DEPTH, N_FOX), f32, 1.0, 4.0),
        "diff_lq1": 0.1 * jax.random.normal(ks[8], (DEPTH, HEAD_DIM), f32),
        "diff_lk1": 0.1 * jax.random.normal(ks[9], (DEPTH, HEAD_DIM), f32),
        "diff_lq2": 0.1 * jax.random.normal(ks[10], (DEPTH, HEAD_DIM), f32),
        "diff_lk2": 0.1 * jax.random.normal(ks[11], (DEPTH, HEAD_DIM), f32),
        "diff_subln": gain(ks[12], (DEPTH, DIFF_V)),
        "proj_a": nrm(ks[13], (DEPTH, W_A, D_MODEL), W_A),
        "proj_b": nrm(ks[14], (DEPTH, W_B, D_MODEL), W_B),
        "proj_c": nrm(ks[15], (DEPTH, W_C, D_MODEL), W_C),
        "w_out": nrm(ks[16], (DEPTH, D_MODEL, D_MODEL), D_MODEL),
        "ffn2_norm": gain(ks[17], (DEPTH, D_MODEL)),
        "ffn2_w1": nrm(ks[18], (DEPTH, D_MODEL, D_FF), D_MODEL),
        "ffn2_w3": nrm(ks[19], (DEPTH, D_MODEL, D_FF), D_MODEL),
        "ffn2_w2": nrm(ks[20], (DEPTH, D_FF, D_MODEL), D_FF),
        "final_norm": gain(ks[21], (D_MODEL,)),
    }

def reference(x, ffn1_norm, ffn1_w1, ffn1_w3, ffn1_w2, mix_norm, w_in, forget_bias,
              diff_lq1, diff_lk1, diff_lq2, diff_lk2, diff_subln, proj_a, proj_b, proj_c,
              w_out, ffn2_norm, ffn2_w1, ffn2_w3, ffn2_w2, final_norm):
    split_idx = np.cumsum(IN_SIZES)[:-1].tolist()
    h = x
    b, s, _ = x.shape
    for l in range(DEPTH):
        h = h + 0.5 * _swiglu(_rmsnorm(h, ffn1_norm[l]), ffn1_w1[l], ffn1_w3[l], ffn1_w2[l])

        u = _rmsnorm(h, mix_norm[l])
        z = u @ w_in[l]
        (a_q, a_k, a_v, b_q, b_k, b_v, b_f, c_q, c_k, c_v, g) = jnp.split(z, split_idx, axis=-1)
        lam_init = 0.8 - 0.6 * math.exp(-0.3 * l)
        o_a = _diff_attention(a_q, a_k, a_v, diff_lq1[l], diff_lk1[l], diff_lq2[l],
                              diff_lk2[l], diff_subln[l], lam_init)
        o_b = _forgetting_attention(b_q, b_k, b_v, b_f, forget_bias[l])
        o_c = _stick_breaking_attention(c_q, c_k, c_v)
        gates = jax.nn.sigmoid(g.reshape(b, s, N_BRANCH, D_MODEL))
        m = (gates[:, :, 0] * (o_a @ proj_a[l])
             + gates[:, :, 1] * (o_b @ proj_b[l])
             + gates[:, :, 2] * (o_c @ proj_c[l]))
        h = h + m @ w_out[l]

        h = h + 0.5 * _swiglu(_rmsnorm(h, ffn2_norm[l]), ffn2_w1[l], ffn2_w3[l], ffn2_w2[l])
    return _rmsnorm(h, final_norm)


_drawn_inputs = setup_inputs


def setup_inputs(seed=0):
    import zlib

    import numpy as np

    out = dict(_drawn_inputs(seed))
    spreads = {}
    factors = {'diff_lq1': 3.531, 'diff_lk2': 3.203}
    for name, (base, spread) in spreads.items():
        noise = np.random.default_rng([zlib.crc32(name.encode()), seed]).standard_normal(out[name].shape)
        drawn = base * np.exp(spread * noise) if base else spread * noise
        out[name] = __import__('jax').numpy.asarray(drawn.astype(out[name].dtype))
    for name, factor in factors.items():
        out[name] = (out[name] * factor).astype(out[name].dtype)
    return out
```

```python
from contextlib import ExitStack, contextmanager
import math

import numpy as np
import concourse.bass as bass
from concourse import mybir

F32 = mybir.dt.float32
F32R = mybir.dt.float32r
F16 = mybir.dt.float16
ACT = mybir.ActivationFunctionType
ALU = mybir.AluOpType
AX_X = mybir.AxisListType.X

P = 128
D_MODEL, SEQ, DEPTH, D_FF = 1024, 512, 2, 2816
HEAD = 64
N_DIFF, N_FOX, N_SB = 4, 8, 8
EPS, SUBLN_EPS = 1e-6, 1e-5
ND = D_MODEL // P
NF = D_FF // P
NQ = SEQ // P
NT = 4
SCALE = 1.0 / math.sqrt(HEAD)
LN_EXP = "natural_log_exp_and_others"
NEG = -1.0e30

UNIT = 8
SLOTS = 3
FFN_A_UNITS = 2 * NF + 1
W2_UNITS = 3
HEAD_UNITS = 9
TAIL_UNITS = 9
OUT_UNITS = ND + 1
LAYER_UNITS = 2 * (FFN_A_UNITS + W2_UNITS * ND) + HEAD_UNITS * NT + TAIL_UNITS * ND // 2 + OUT_UNITS
N_UNITS = DEPTH * LAYER_UNITS
assert LAYER_UNITS % SLOTS == 0 and FFN_A_UNITS % SLOTS == 0 and OUT_UNITS % SLOTS == 0

Q_OFF = [P * i * (i + 1) // 2 for i in range(NQ)]
K_OFF = [P * (j * NQ - j * (j - 1) // 2) for j in range(NQ)]
TRI = P * NQ * (NQ + 1) // 2
PT_OFF = K_OFF[:-1] + [K_OFF[-1] + P]
PT_SIZE = TRI + P
WIDE = 2 * P

GAINS = 3 * DEPTH + 1
P_GAIN = 0
P_SUBLN = P_GAIN + GAINS * ND
P_FB = P_SUBLN + DEPTH
P_WF = P_FB + DEPTH
P_END = P_WF + DEPTH * ND * N_FOX
C_IDENT, C_STRICT01, C_ONES, C_SEL = 0, P, 2 * P, 3 * P
C_MASK = C_SEL + N_FOX + N_DIFF
C_EPS = C_MASK + 4
C_END = C_EPS + 2
R_IDENT, R_CAUSAL, R_STRICT, R_NEGTRI, R_NEGONES, ROUNDED = 0, 2, 4, 6, 7, 8


def lam_init(layer):
    return 0.8 - 0.6 * math.exp(-0.3 * layer)


class Counts:

    def __init__(self, eng, sems):
        self.eng = eng
        self.reg, self.more, self.base = {}, {}, {}
        for s in sems:
            self.reg[s] = eng.alloc_register(f"count_{len(self.reg)}_{eng.engine}".replace(".", "_"))
            eng.reg_mov(self.reg[s], 0)
            self.more[s], self.base[s] = 0, 0

    def value(self, sem, ahead=0):
        if self.base[sem] is None:
            self.base[sem] = self.eng.snap(self.reg[sem])
        return self.base[sem] + (self.more[sem] + ahead)

    def skip(self, sem, n=1):
        self.more[sem] += n

    def next(self, sem, n=1):
        self.more[sem] += n
        return self.value(sem)

    def peek(self, sem, n=1):
        return self.value(sem, n)

    def fold(self):
        for s, n in self.more.items():
            if n:
                self.eng.reg_add(self.reg[s], self.reg[s], n)
            self.more[s] = 0
            self.base[s] = None

    def read(self):
        for s in self.reg:
            self.base[s] = self.eng.snap(self.reg[s])

    @contextmanager
    def turns(self, first, last):
        self.fold()
        with self.eng.Fori(first, last) as i:
            self.read()
            yield i
            self.fold()
        self.read()


def trunk(nc, x, stream, params, lambdas, const, const_r, const_b, out):
    ctx = ExitStack()
    with ctx:
        def sb(name, cols, dt=F32):
            return ctx.enter_context(nc.sbuf_tensor(name, [P, cols], dt))

        h = sb("h", ND * SEQ)
        u_hi = sb("u_hi", ND * SEQ, F32R)
        u_lo = sb("u_lo", ND * SEQ, F32R)
        w_raw = sb("w_raw", SLOTS * UNIT * P)
        w_hi = sb("w_hi", SLOTS * UNIT * P, F32R)
        w_lo = sb("w_lo", SLOTS * UNIT * P, F32R)
        rstd = sb("rstd", SEQ)
        area = sb("area", NF * 2 * SEQ + WIDE, F32R)
        v_area = sb("v_area", 5120, F32R)
        scratch = sb("scratch", 8 * SEQ)
        bias_l = sb("bias_l", SEQ)
        base_l = sb("base_l", SEQ, F16)
        base_r = sb("base_r", SEQ, F16)
        cst = sb("cst", C_END)
        cst_r = sb("cst_r", ROUNDED * P, F32R)
        par = sb("par", P_END)
        lam = sb("lam", 16)
        stat = sb("stat", 32)

        ident, strict01, ones = (cst[:, c:c + P] for c in (C_IDENT, C_STRICT01, C_ONES))
        ident_r, negtri_r, negones_r = (cst_r[:, k * P:(k + 1) * P] for k in (R_IDENT, R_NEGTRI, R_NEGONES))

        def masked(which, last):
            return cst_r[:, (which - last) * P:(which - last + 2) * P]


        def g_hi(f):
            return area[:, f * 2 * SEQ:f * 2 * SEQ + SEQ]

        def g_lo(f):
            return area[:, f * 2 * SEQ + SEQ:(f + 1) * 2 * SEQ]

        O_HI, O_LO = 0, 3 * NT * SEQ
        QK = 2 * O_LO
        PT_HI = QK + 3 * 4 * SEQ
        PT_LO = PT_HI + PT_SIZE
        L_ROWS = PT_LO + PT_SIZE
        R_ROWS = L_ROWS + 2 * SEQ
        AREA = R_ROWS + SEQ
        assert AREA >= NF * 2 * SEQ
        M_HI, M_LO = QK, QK + ND * SEQ

        def qk(branch, which):
            at = QK + (branch * 4 + which) * SEQ
            return area[:, at:at + SEQ]

        bias_r = area[:, R_ROWS:R_ROWS + SEQ]

        def l_rows(slot):
            return area[:, L_ROWS + slot * SEQ:L_ROWS + (slot + 1) * SEQ]

        V_AT = {0: 0, 1: 1024, 2: 3072}

        def val(branch, head, part):
            at = V_AT[branch] + (head * 2 + part) * SEQ
            return v_area[:, at:at + SEQ]

        def tile(k):
            return scratch[:, k * SEQ:(k + 1) * SEQ]

        prob = [scratch[:, 2 * SEQ:2 * SEQ + TRI], scratch[:, 2 * SEQ + TRI:2 * SEQ + 2 * TRI]]
        acc = tile(7)

        ps = ctx.enter_context(nc.psum_tensor("ps", [P, 8, SEQ], F32))
        AUX, OB, SB0 = 2, 3, 4

        def slot(w, k, b=0):
            return w[:, (k * UNIT + b) * P:(k * UNIT + b + 1) * P]

        def sem(name):
            return ctx.enter_context(nc.semaphore(name))

        small_landed = sem("small_landed")
        const_set = sem("const_set")
        landed = [sem(f"landed{k}") for k in range(SLOTS)]
        w_hi_set = sem("w_hi_set")
        w_set = sem("w_set")
        unit_done = sem("unit_done")
        vec_done = sem("vec_done")
        act_done = sem("act_done")
        h_set = sem("h_set")
        hg_set = sem("hg_set")
        sq_set = sem("sq_set")
        acc_set = sem("acc_set")
        u_hi_set = sem("u_hi_set")
        u_set = sem("u_set")
        ms_set = sem("ms_set")
        rstd_set = sem("rstd_set")
        gate_in = sem("gate_in")
        gate_out = sem("gate_out")
        up_set = sem("up_set")
        hid_set = sem("hid_set")
        g_hi_set = sem("g_hi_set")
        g_set = sem("g_set")
        lam_in = sem("lam_in")
        lam_out = sem("lam_out")
        wf_hi_set = sem("wf_hi_set")
        wf_set = sem("wf_set")
        forget_mm = sem("forget_mm")
        forget_in = sem("forget_in")
        forget_out = sem("forget_out")
        staged = sem("staged")
        qk_hi_set = sem("qk_hi_set")
        qk_set = sem("qk_set")
        turned = sem("turned")
        v_hi_set = sem("v_hi_set")
        v_set = sem("v_set")
        rows_set = sem("rows_set")
        score_set = sem("score_set")
        max_set = sem("max_set")
        exp_set = sem("exp_set")
        prob_set = sem("prob_set")
        probs_turned = sem("probs_turned")
        log_set = sem("log_set")
        sp_set = sem("sp_set")
        pt_hi_set = sem("pt_hi_set")
        pt_set = sem("pt_set")
        stick_set = sem("stick_set")
        o_mm = sem("o_mm")
        o_sq = sem("o_sq")
        o_ms = sem("o_ms")
        o_rstd = sem("o_rstd")
        o_norm = sem("o_norm")
        o_hi_set = sem("o_hi_set")
        o_set = sem("o_set")
        proj_mm = sem("proj_mm")
        tail_read = sem("tail_read")
        m_mid = sem("m_mid")
        m_hi_set = sem("m_hi_set")
        m_set = sem("m_set")
        y_set = sem("y_set")
        stored = [sem(f"stored{k}") for k in range(2)]

        block = ctx.enter_context(nc.Block())

        @block.sync
        def _(sp):
            sp.dma_start(h[:], x).then_inc(small_landed, 16)
            sp.dma_start(cst[:], const).then_inc(small_landed, 16)
            sp.dma_start(par[:], params).then_inc(small_landed, 16)
            sp.dma_start(scratch[:, 0:ROUNDED * P], const_r).then_inc(small_landed, 16)
            sp.dma_start(scratch[:, 1024:1024 + 2 * SEQ], const_b).then_inc(small_landed, 16)
            sp.dma_start(scratch[:, 5 * SEQ:6 * SEQ], lambdas).then_inc(small_landed, 16)
            counts = Counts(sp, [w_set])

            def load(unit, k):
                sp.dma_start(w_raw[:, k * UNIT * P:(k + 1) * UNIT * P], stream[unit, :, :]).then_inc(landed[k], 16)

            for k in range(SLOTS):
                load(k, k)
            with counts.turns(0, N_UNITS // SLOTS) as i:
                for k in range(SLOTS):
                    sp.wait_ge(w_set, counts.next(w_set))
                    sp.dma_start(w_raw[:, k * UNIT * P:(k + 1) * UNIT * P],
                                 stream[bass.ds(i * SLOTS + SLOTS + k, 1), :, :].rearrange("a p n -> p (a n)")
                                 ).then_inc(landed[k], 16)
            for d in range(ND):
                sp.wait_ge(y_set, d + 1)
                sp.dma_start(out[d, :, :], tile(d % 2)).then_inc(stored[d % 2], 16)
            for k in range(2):
                sp.wait_ge(stored[k], 16 * ND // 2)
            for k in range(SLOTS):
                sp.wait_ge(landed[k], 16 * (N_UNITS // SLOTS + 1))

        @block.tensor
        def _(pe):
            c = Counts(pe, [w_set, u_set, acc_set, rstd_set, up_set, g_set, h_set, wf_set, staged,
                            rows_set, qk_set, v_set, exp_set, prob_set, pt_set, o_sq, o_rstd, o_set,
                            tail_read, m_set])

            def three(dst, hi, lo, x_hi, x_lo, start, stop, **kw):
                pe.matmul(dst, hi, x_hi, start=start, stop=False, **kw)
                pe.matmul(dst, hi, x_lo, start=False, stop=False, **kw)
                return pe.matmul(dst, lo, x_hi, start=False, stop=stop, **kw)

            def u(k):
                return u_hi[:, k * SEQ:(k + 1) * SEQ], u_lo[:, k * SEQ:(k + 1) * SEQ]

            def u_unit(bank, k, first=False):
                pe.wait_ge(w_set, c.next(w_set))
                for b in range(UNIT):
                    if first:
                        pe.wait_ge(u_set, c.next(u_set))
                    last = three(ps[:, bank, :], slot(w_hi, k, b), slot(w_lo, k, b), *u(b),
                                 start=b == 0, stop=b == UNIT - 1)
                return last

            def sum_of_squares():
                pe.wait_ge(acc_set, c.next(acc_set, ND))
                pe.matmul(ps[:, 7, :], ones, acc, start=True, stop=True).then_inc(ms_set, 1)

            def ffn():
                pe.wait_ge(u_set, c.next(u_set, ND))
                with c.turns(0, NF // 3) as _i:
                    for f in range(3):
                        pe.wait_ge(up_set, c.next(up_set))
                        u_unit(2 * f, 2 * f % SLOTS).then_inc(unit_done, 1)
                        u_unit(2 * f + 1, (2 * f + 1) % SLOTS).then_inc(unit_done, 1)
                pe.wait_ge(up_set, c.next(up_set))
                u_unit(0, 0).then_inc(unit_done, 1)
                u_unit(1, 1).then_inc(unit_done, 2)
                c.skip(w_set)
                pe.wait_ge(rstd_set, c.next(rstd_set))
                with c.turns(0, ND // 2) as _i:
                    for d in range(2):
                        pe.wait_ge(h_set, c.next(h_set))
                        for k in range(W2_UNITS):
                            pe.wait_ge(w_set, c.next(w_set))
                            for b in range(min(UNIT, NF - k * UNIT)):
                                f = k * UNIT + b
                                if f == 0:
                                    pe.wait_ge(g_set, c.peek(g_set, NF - 3))
                                elif f >= NF - 3:
                                    pe.wait_ge(g_set, c.peek(g_set, f + 1))
                                last = three(ps[:, 6 + d, :], slot(w_hi, k, b), slot(w_lo, k, b),
                                             g_hi(f), g_lo(f), start=f == 0, stop=f == NF - 1)
                            last.then_inc(unit_done, 1)
                c.skip(g_set, NF)
                sum_of_squares()

            def forget():
                pe.wait_ge(wf_set, c.next(wf_set))
                for k in range(ND):
                    at = PT_HI + k * P
                    last = three(ps[:, AUX, :], area[:, at:at + P], area[:, at + ND * P:at + ND * P + P], *u(k),
                                 start=k == 0, stop=k == ND - 1)
                last.then_inc(forget_mm, 1)
                pe.wait_ge(rstd_set, c.next(rstd_set))

            def scores(branch, half, rows):
                a = slice(half * HEAD, (half + 1) * HEAD)
                q_hi, q_lo, k_hi, k_lo = (qk(branch, w)[a, :] for w in range(4))
                for i in range(NQ):
                    n, m = max(WIDE, (i + 1) * P), slice(i * P, (i + 1) * P)
                    dst = ps[:, SB0 + i, 0:n]
                    pe.matmul(dst, q_hi[:, m], k_hi[:, 0:n], start=True, stop=False)
                    pe.matmul(dst, q_hi[:, m], k_lo[:, 0:n], start=False, stop=False)
                    pe.matmul(dst, q_lo[:, m], k_hi[:, 0:n], start=False, stop=False)
                    pe.matmul(dst, l_rows(rows)[:, m], bias_r[:, 0:n], start=False, stop=False)
                    pe.matmul(ps[:, SB0 + i, n - WIDE:n], ident_r, masked(R_CAUSAL, last=i > 0), start=False,
                              stop=True).then_inc(score_set, 1)

            def turn_probs(buf):
                for i in range(NQ):
                    pe.wait_ge(prob_set, c.next(prob_set))
                    for j in range(i + 1):
                        at = Q_OFF[i] + j * P
                        last = pe.transpose(ps[:, SB0 + j, (i - j) * P:(i - j + 1) * P], prob[buf][:, at:at + P], ident)
                last.then_inc(probs_turned, 1)

            def turn_values(st):
                for j in range(NQ):
                    last = pe.transpose(ps[:, AUX, j * P:(j + 1) * P], tile(st)[:, j * P:(j + 1) * P], ident)
                last.then_inc(turned, 1)

            def wide_keys(j):
                n = max(WIDE, (NQ - j) * P)
                end = PT_OFF[j] + (NQ - j) * P
                return n, area[:, PT_HI + end - n:PT_HI + end], area[:, PT_LO + end - n:PT_LO + end]

            def weighted(branch, head, first, final):
                if first:
                    pe.wait_ge(v_set, c.next(v_set))
                    pe.wait_ge(o_set, c.next(o_set))
                for j in range(NQ):
                    pe.wait_ge(pt_set, c.next(pt_set))
                    v_hi, v_lo = (val(branch, head, p)[:, j * P:(j + 1) * P] for p in range(2))
                    n, w_hi_j, w_lo_j = wide_keys(j)
                    last = three(ps[:, OB, SEQ - n:SEQ], v_hi, v_lo, w_hi_j, w_lo_j,
                                 start=first and j == 0, stop=final and j == NQ - 1)
                if final:
                    last.then_inc(o_mm, 1)

            def stick_scores(half):
                a = slice(half * HEAD, (half + 1) * HEAD)
                q_hi, q_lo, k_hi, k_lo = (qk(2, w)[a, :] for w in range(4))
                for j in range(NQ):
                    m, n = slice(j * P, (j + 1) * P), max(WIDE, (NQ - j) * P)
                    three(ps[:, SB0 + j, 0:n], k_hi[:, m], k_lo[:, m], q_hi[:, SEQ - n:], q_lo[:, SEQ - n:],
                          start=True, stop=True).then_inc(score_set, 1)

            def stick_sums():
                pe.wait_ge(pt_set, c.next(pt_set, NQ))
                for j in range(NQ):
                    width = max(WIDE, (NQ - j) * P)
                    for i in range(j, NQ):
                        n, *parts = wide_keys(i)
                        for part in parts:
                            pe.matmul(ps[:, SB0 + j, width - n:width], negtri_r if i == j else negones_r, part,
                                      start=False, stop=False, skip_group_check=True)
                    pe.matmul(ps[:, SB0 + j, 0:WIDE], ident_r, masked(R_STRICT, last=j == NQ - 1), start=False,
                              stop=True, skip_group_check=True).then_inc(stick_set, 1)

            def diff_norm():
                pe.wait_ge(o_sq, c.next(o_sq))
                pe.matmul(ps[:, AUX, :], ones, tile(7), start=True, stop=True).then_inc(o_ms, 1)
                pe.wait_ge(o_rstd, c.next(o_rstd))

            def unit(k):
                u_unit(k % 2, k % SLOTS).then_inc(unit_done, 1)

            def heads(diff_before):
                if diff_before:
                    pe.wait_ge(rows_set, c.next(rows_set))
                    scores(0, 0, 0)
                unit(0)
                if diff_before:
                    pe.wait_ge(exp_set, c.next(exp_set, NQ))
                    scores(0, 1, 0)
                unit(1)
                if diff_before:
                    c.skip(exp_set, NQ)
                    turn_probs(0)
                pe.wait_ge(staged, c.next(staged))
                unit(2)
                if diff_before:
                    weighted(0, 0, True, True)
                pe.wait_ge(qk_set, c.next(qk_set, 2))
                stick_scores(0)
                pe.wait_ge(staged, c.next(staged))
                unit(3)
                if diff_before:
                    diff_norm()
                pe.wait_ge(staged, c.next(staged))
                turn_values(0)
                stick_sums()
                unit(4)
                weighted(2, 0, True, False)
                stick_scores(1)
                pe.wait_ge(staged, c.next(staged))
                unit(5)
                stick_sums()
                pe.wait_ge(staged, c.next(staged))
                unit(6)
                weighted(2, 1, False, True)
                pe.wait_ge(rows_set, c.next(rows_set))
                pe.wait_ge(qk_set, c.next(qk_set, 2))
                scores(1, 0, 0)
                pe.wait_ge(staged, c.next(staged))
                turn_values(1)
                unit(7)
                turn_probs(0)
                pe.wait_ge(staged, c.next(staged))
                unit(8)
                weighted(1, 0, True, False)
                pe.wait_ge(rows_set, c.next(rows_set))
                scores(1, 1, 1)
                pe.wait_ge(staged, c.next(staged, 2))
                turn_values(0)
                turn_probs(1)
                weighted(1, 1, False, True)
                c.skip(exp_set, 2 * NQ)
                pe.wait_ge(qk_set, c.next(qk_set, 2))

            def mixer():
                pe.wait_ge(u_set, c.next(u_set, ND))
                forget()
                heads(False)
                with c.turns(1, NT) as _t:
                    heads(True)
                pe.wait_ge(rows_set, c.next(rows_set))
                scores(0, 0, 0)
                pe.wait_ge(exp_set, c.next(exp_set, NQ))
                scores(0, 1, 0)
                c.skip(exp_set, NQ)
                turn_probs(0)
                weighted(0, 0, True, True)
                diff_norm()
                tail()

            def branch_products(k0, b0, banks, waits):
                for branch in range(3):
                    pe.wait_ge(tail_read, c.peek(tail_read, waits[branch]))
                    for k in range(NT):
                        b = b0 + branch * NT + k
                        s, b = (k0 + b // UNIT) % SLOTS, b % UNIT
                        if b == 0:
                            pe.wait_ge(w_set, c.next(w_set))
                        at = (branch * NT + k) * SEQ
                        last = three(ps[:, banks[branch], :], slot(w_hi, s, b), slot(w_lo, s, b),
                                     area[:, O_HI + at:O_HI + at + SEQ], area[:, O_LO + at:O_LO + at + SEQ],
                                     start=k == 0, stop=k == NT - 1)
                        if b == UNIT - 1 or k == NT - 1:
                            last.then_inc(unit_done if b == UNIT - 1 else proj_mm, 1)

            def tail():
                pe.wait_ge(o_set, c.peek(o_set, 1))
                with c.turns(0, ND // 2) as _i:
                    for k in range(3):
                        pe.wait_ge(tail_read, c.peek(tail_read, 7 + k))
                        u_unit(k, k).then_inc(unit_done, 1)
                    branch_products(0, 0, (3, 4, 5), (4, 12, 6))
                    branch_products(1, 4, (6, 7, 4), (10, 11, 12 + 5))
                    for k in range(3):
                        pe.wait_ge(tail_read, c.peek(tail_read, 12 + 1 + k))
                        u_unit(k, k).then_inc(unit_done, 1)
                    c.skip(tail_read, 12)
                pe.wait_ge(tail_read, c.peek(tail_read, 10))
                pe.wait_ge(tail_read, c.peek(tail_read, 11))
                for d in range(ND):
                    pe.wait_ge(h_set, c.next(h_set))
                    pe.wait_ge(w_set, c.next(w_set))
                    for b in range(UNIT):
                        if d == 0:
                            pe.wait_ge(m_set, c.next(m_set))
                        last = three(ps[:, 6 + d % 2, :], slot(w_hi, d % SLOTS, b), slot(w_lo, d % SLOTS, b),
                                     area[:, M_HI + b * SEQ:M_HI + (b + 1) * SEQ],
                                     area[:, M_LO + b * SEQ:M_LO + (b + 1) * SEQ], start=b == 0, stop=b == UNIT - 1)
                    last.then_inc(unit_done, 1 if d < ND - 1 else 2)
                c.skip(w_set)
                sum_of_squares()

            pe.wait_ge(small_landed, 16 * 6)
            pe.wait_ge(const_set, 2)
            sum_of_squares()
            with c.turns(0, DEPTH) as _l:
                ffn()
                mixer()
                ffn()

        HG, SQ = tile(4), tile(5)
        wf_bank = area[:, PT_HI:PT_HI + 2 * ND * P]

        def neg_max(buf, i):
            return stat[:, 4 * buf + i:4 * buf + i + 1]

        def total(buf, i):
            return stat[:, 8 + 4 * buf + i:9 + 4 * buf + i]

        def inverse(buf, i):
            return stat[:, 16 + 4 * buf + i:17 + 4 * buf + i]

        def wf_source(layer, k):
            at = P_WF + layer * (ND * N_FOX) + k * N_FOX
            return par[:, bass.ds(at, N_FOX)].unsqueeze(1).broadcast_to([P, P // N_FOX, N_FOX])

        def keys(part, j):
            return area[:, part + PT_OFF[j]:part + PT_OFF[j] + (NQ - j) * P]

        def stick_bank(j):
            spare = P if j == NQ - 1 else 0
            return ps[:, SB0 + j, spare:spare + (NQ - j) * P]

        def key_block(buf, j):
            return prob[buf][:, K_OFF[j]:K_OFF[j] + (NQ - j) * P]

        def query_block(buf, i):
            return prob[buf][:, Q_OFF[i]:Q_OFF[i] + (i + 1) * P]

        def half_tile(ap, hd):
            return ap.rearrange("p (j e) -> p j e", j=NQ)[:, :, hd * HEAD:(hd + 1) * HEAD]

        @block.scalar
        def _(act):
            c = Counts(act, [*landed, unit_done, act_done, h_set, hg_set, ms_set, gate_in, hid_set, forget_in,
                             staged, turned, score_set, max_set, probs_turned, sp_set, stick_set, o_mm, o_ms,
                             o_norm, tail_read, m_mid])

            def hi(dst, src):
                return act.activation(dst, src, ACT.Copy)

            def split(k, after=True):
                if after:
                    act.wait_ge(unit_done, c.next(unit_done))
                act.wait_ge(landed[k], c.next(landed[k], 16))
                hi(w_hi[:, k * UNIT * P:(k + 1) * UNIT * P], w_raw[:, k * UNIT * P:(k + 1) * UNIT * P]
                   ).then_inc(w_hi_set, 1)

            def follow(at, changed=True):
                first = h_set if changed else hg_set
                act.wait_ge(first, c.next(first))
                act.activation(SQ, h[:, bass.ds(at, SEQ)], ACT.Square).then_inc(sq_set, 1)
                if changed:
                    act.wait_ge(hg_set, c.next(hg_set))
                hi(u_hi[:, bass.ds(at, SEQ)], HG).then_inc(u_hi_set, 1)

            def norm():
                act.preload_act_table_set(LN_EXP)
                act.wait_ge(ms_set, c.next(ms_set))
                act.activation(rstd[:], ps[:, 7, :], ACT.Ln, bias=cst[:, C_EPS:C_EPS + 1],
                               scale=1.0 / D_MODEL).then_inc(act_done, 1)
                act.wait_ge(act_done, c.next(act_done))
                act.activation(rstd[:], rstd[:], ACT.Exp, scale=-0.5).then_inc(rstd_set, 1)

            def hidden(at, k0, k1):
                split(k0)
                act.wait_ge(gate_in, c.next(gate_in))
                act.activation(tile(2), tile(0), ACT.Silu).then_inc(gate_out, 1)
                split(k1)
                act.wait_ge(hid_set, c.next(hid_set))
                hi(area[:, bass.ds(at, SEQ)], tile(3)).then_inc(g_hi_set, 1)

            def ffn():
                norm()
                act.preload_act_table(ACT.Silu)
                with c.turns(0, NF // 3) as i:
                    for f in range(3):
                        hidden((i * 3 + f) * (2 * SEQ), 2 * f % SLOTS, (2 * f + 1) % SLOTS)
                hidden((NF - 1) * 2 * SEQ, 0, 1)
                split(2)
                with c.turns(0, ND // 2) as i:
                    for d in range(2):
                        for k in range(W2_UNITS):
                            split(k)
                        follow((i * 2 + d) * SEQ)

            def forget(layer):
                for k in range(ND):
                    dst = wf_bank[:, k * P:(k + 1) * P].rearrange("p (r n) -> p r n", n=N_FOX)
                    last = hi(dst, wf_source(layer, k))
                last.then_inc(wf_hi_set, 1)
                norm()
                act.wait_ge(forget_in, c.next(forget_in))
                act.activation(tile(2), tile(0), ACT.Abs).then_inc(act_done, 1)
                act.wait_ge(act_done, c.next(act_done))
                act.activation(tile(2), tile(2), ACT.Exp, scale=-1.0).then_inc(act_done, 1)
                act.wait_ge(act_done, c.next(act_done))
                act.activation(tile(2), tile(2), ACT.Ln, bias=1.0).then_inc(forget_out, 1)
                act.wait_ge(forget_in, c.next(forget_in))
                hi(l_rows(1), tile(1)).then_inc(forget_out, 1)

            def split_qk(branch, which, k):
                act.wait_ge(staged, c.next(staged))
                hi(qk(branch, which), tile(k % 2)).then_inc(qk_hi_set, 1)
                split(k % SLOTS)

            def exps(buf):
                for i in range(NQ):
                    act.wait_ge(max_set, c.next(max_set))
                    act.activation(query_block(buf, i), ps[:, SB0 + i, 0:(i + 1) * P], ACT.Exp,
                                   bias=neg_max(buf, i), accum_out=total(buf, i)).then_inc(exp_set, 1)

            def turned_hi():
                act.wait_ge(probs_turned, c.next(probs_turned))
                for j in range(NQ):
                    hi(keys(PT_HI, j), ps[:, SB0 + j, 0:(NQ - j) * P]).then_inc(pt_hi_set, 1)

            def stick_logs():
                for step in range(NQ + 2):
                    if step < NQ:
                        act.wait_ge(score_set, c.next(score_set))
                        act.activation(key_block(0, step), stick_bank(step), ACT.Abs).then_inc(act_done, 1)
                    if 0 <= step - 1 < NQ:
                        act.wait_ge(act_done, c.next(act_done))
                        k = key_block(0, step - 1)
                        act.activation(k, k, ACT.Exp, scale=-1.0).then_inc(act_done, 1)
                    if 0 <= step - 2 < NQ:
                        act.wait_ge(act_done, c.next(act_done))
                        act.activation(key_block(1, step - 2), key_block(0, step - 2), ACT.Ln, bias=1.0
                                       ).then_inc(log_set, 1)
                for j in range(NQ):
                    act.wait_ge(sp_set, c.next(sp_set))
                    hi(keys(PT_HI, j), key_block(1, j)).then_inc(pt_hi_set, 1)

            def stick_weights():
                for j in range(NQ):
                    act.wait_ge(stick_set, c.next(stick_set))
                    act.activation(key_block(0, j), stick_bank(j), ACT.Exp).then_inc(act_done, 1)
                for j in range(NQ):
                    act.wait_ge(act_done, c.next(act_done))
                    hi(keys(PT_HI, j), key_block(0, j)).then_inc(pt_hi_set, 1)

            def values_hi(branch):
                act.wait_ge(turned, c.next(turned))
                if branch == 0:
                    hi(val(0, 0, 0), ps[:, AUX, :]).then_inc(v_hi_set, 1)
                else:
                    for hd in range(2):
                        hi(half_tile(val(branch, hd, 0), hd), half_tile(ps[:, AUX, :], hd)).then_inc(v_hi_set, 1)

            def output_hi(branch, t):
                at = (t + branch * NT) * SEQ + O_HI
                if branch == 0:
                    act.wait_ge(o_norm, c.next(o_norm))
                    hi(area[:, bass.ds(at, SEQ)], tile(7)).then_inc(o_hi_set, 1)
                else:
                    act.wait_ge(o_mm, c.next(o_mm))
                    hi(area[:, bass.ds(at, SEQ)], ps[:, OB, :]).then_inc(o_hi_set, 1)

            def output_square():
                act.wait_ge(o_mm, c.next(o_mm))
                act.activation(tile(7), ps[:, OB, :], ACT.Square).then_inc(o_sq, 1)

            def output_rstd():
                act.wait_ge(o_ms, c.next(o_ms))
                act.activation(tile(7), ps[:, AUX, :], ACT.Ln, bias=cst[:, C_EPS + 1:C_EPS + 2],
                               scale=1.0 / (2 * HEAD)).then_inc(act_done, 1)
                act.wait_ge(act_done, c.next(act_done))
                act.activation(tile(7), tile(7), ACT.Exp, scale=-0.5).then_inc(o_rstd, 1)

            def heads(t, diff_before):
                if diff_before:
                    c.skip(score_set, NQ)
                    exps(0)
                split_qk(2, 0, 0)
                if diff_before:
                    c.skip(score_set, NQ)
                    exps(1)
                split_qk(2, 2, 1)
                if diff_before:
                    turned_hi()
                c.skip(staged)
                split(2)
                if diff_before:
                    output_square()
                stick_logs()
                split_qk(1, 0, 3)
                if diff_before:
                    output_rstd()
                values_hi(2)
                stick_weights()
                if diff_before:
                    output_hi(0, t - 1)
                split_qk(1, 2, 4)
                stick_logs()
                c.skip(staged)
                split(2)
                stick_weights()
                split_qk(0, 0, 6)
                output_hi(2, t)
                c.skip(score_set, NQ)
                exps(0)
                values_hi(1)
                split_qk(0, 2, 7)
                turned_hi()
                c.skip(staged)
                split(2)
                c.skip(score_set, NQ)
                exps(1)
                values_hi(0)
                turned_hi()
                output_hi(1, t)

            def mixer(layer):
                forget(layer)
                heads(0, False)
                with c.turns(1, NT) as t:
                    heads(t, True)
                c.skip(score_set, 2 * NQ)
                exps(0)
                exps(1)
                turned_hi()
                output_square()
                output_rstd()
                output_hi(0, NT - 1)

                def gates():
                    for k in range(3):
                        split(k)
                        act.wait_ge(tail_read, c.next(tail_read))
                        act.activation(tile(1 + k), tile(6 * (k % 2)), ACT.Sigmoid).then_inc(gate_out, 1)
                    c.skip(tail_read, 3)

                def mixed_hi(at):
                    act.wait_ge(m_mid, c.next(m_mid))
                    hi(area[:, bass.ds(at, SEQ)], tile(4)).then_inc(m_hi_set, 1)

                act.preload_act_table(ACT.Sigmoid)
                with c.turns(0, ND // 2) as i:
                    gates()
                    split(0)
                    mixed_hi(i * (2 * SEQ) + M_HI)
                    split(1)
                    split(2)
                    gates()
                    mixed_hi(i * (2 * SEQ) + (M_HI + SEQ))
                for d in range(ND):
                    split(d % SLOTS)
                    follow(d * SEQ)
                split(2)

            act.wait_ge(small_landed, 16 * 6)
            hi(cst_r[:], scratch[:, 0:ROUNDED * P]).then_inc(const_set, 1)
            act.wait_ge(lam_in, 1)
            act.activation(lam[:, 4:8], lam[:, 8:12], ACT.Exp).then_inc(lam_out, 1)
            c.skip(h_set, 2)
            c.skip(tail_read, 12)
            for k in range(SLOTS):
                split(k, after=False)
            for d in range(ND):
                follow(d * SEQ, changed=False)
            with c.turns(0, DEPTH) as layer:
                ffn()
                mixer(layer)
                ffn()
            norm()

        @block.vector
        def _(dve):
            c = Counts(dve, [w_hi_set, unit_done, vec_done, h_set, sq_set, acc_set, u_hi_set, rstd_set, gate_out,
                             gate_in, up_set, g_hi_set, wf_hi_set, forget_mm, forget_in, forget_out, qk_hi_set,
                             v_hi_set, score_set, exp_set, log_set, pt_hi_set, o_rstd, o_norm, o_hi_set,
                             proj_mm, tail_read, m_mid, m_hi_set, u_set,
                             prob_set])

            def lo(dst, src, hi_part):
                return dve.tensor_tensor(dst, src, hi_part.bitcast(F32), ALU.subtract)

            def split(k):
                dve.wait_ge(w_hi_set, c.next(w_hi_set))
                at = slice(k * UNIT * P, (k + 1) * UNIT * P)
                lo(w_lo[:, at], w_raw[:, at], w_hi[:, at]).then_inc(w_set, 1)

            def fresh(at, gain, first=False):
                if not first:
                    dve.wait_ge(u_set, c.peek(u_set, 0))
                dve.tensor_scalar(HG, h[:, bass.ds(at, SEQ)], par[:, bass.ds(gain, 1)], None, ALU.mult
                                  ).then_inc(hg_set, 1)
                dve.wait_ge(sq_set, c.next(sq_set))
                dve.tensor_tensor(acc, acc, SQ, ALU.add).then_inc(acc_set, 1)
                dve.wait_ge(acc_set, c.next(acc_set))
                dve.wait_ge(u_hi_set, c.next(u_hi_set))
                lo(u_lo[:, bass.ds(at, SEQ)], HG, u_hi[:, bass.ds(at, SEQ)]).then_inc(u_set, 1)
                c.skip(u_set)

            def update(at, bank, factor, gain):
                dve.scalar_tensor_tensor(h[:, bass.ds(at, SEQ)], ps[:, bank, :], factor,
                                         h[:, bass.ds(at, SEQ)], ALU.mult, ALU.add).then_inc(h_set, 1)
                dve.wait_ge(h_set, c.next(h_set))
                fresh(at, gain)

            def hidden(at, pair, k0, k1):
                a, b, e, v = tile(0), tile(1), tile(2), tile(3)
                dve.wait_ge(unit_done, c.next(unit_done))
                dve.tensor_tensor(a, ps[:, 2 * pair, :], rstd[:], ALU.mult).then_inc(gate_in, 1)
                c.skip(gate_in)
                split(k0)
                dve.wait_ge(unit_done, c.next(unit_done))
                dve.tensor_tensor(b, ps[:, 2 * pair + 1, :], rstd[:], ALU.mult).then_inc(up_set, 1)
                dve.wait_ge(up_set, c.next(up_set))
                dve.wait_ge(gate_out, c.next(gate_out))
                dve.tensor_tensor(v, e, b, ALU.mult).then_inc(hid_set, 1)
                split(k1)
                dve.wait_ge(g_hi_set, c.next(g_hi_set))
                lo(area[:, bass.ds(at + SEQ, SEQ)], v, area[:, bass.ds(at, SEQ)]).then_inc(g_set, 1)

            def ffn(gain):
                dve.wait_ge(rstd_set, c.next(rstd_set))
                with c.turns(0, NF // 3) as i:
                    for f in range(3):
                        hidden((i * 3 + f) * (2 * SEQ), f, 2 * f % SLOTS, (2 * f + 1) % SLOTS)
                hidden((NF - 1) * 2 * SEQ, 0, 0, 1)
                dve.wait_ge(unit_done, c.next(unit_done))
                split(2)
                dve.memset(acc, 0.0).then_inc(vec_done, 1)
                dve.wait_ge(vec_done, c.next(vec_done))
                with c.turns(0, ND // 2) as i:
                    for d in range(2):
                        for k in range(W2_UNITS - 1):
                            dve.wait_ge(unit_done, c.next(unit_done))
                            split(k)
                        dve.wait_ge(unit_done, c.next(unit_done))
                        update((i * 2 + d) * SEQ, 6 + d, 0.5, gain + (i * 2 + d))
                        split(2)

            def forget(layer):
                dve.wait_ge(wf_hi_set, c.next(wf_hi_set))
                for k in range(ND):
                    dst, hi_part = (wf_bank[:, (n + k) * P:(n + k + 1) * P].rearrange("p (r n) -> p r n", n=N_FOX)
                                    for n in (ND, 0))
                    last = lo(dst, wf_source(layer, k), hi_part)
                last.then_inc(wf_set, 1)
                dve.wait_ge(rstd_set, c.next(rstd_set))
                y, soft, neg, run = tile(0), tile(2), tile(3), tile(1)
                dve.wait_ge(forget_mm, c.next(forget_mm))
                for part in (PT_HI, PT_LO):
                    zeros = area[:, part + PT_OFF[-1] - P:part + PT_OFF[-1]]
                    dve.memset(zeros.bitcast(F32), 0.0)
                dve.tensor_tensor(y, ps[:, AUX, :], rstd[:], ALU.mult).then_inc(vec_done, 1)
                dve.wait_ge(vec_done, c.next(vec_done))
                dve.tensor_scalar(y, y, par[:, bass.ds(layer + P_FB, 1)], None, ALU.add).then_inc(forget_in, 1)
                dve.wait_ge(forget_in, c.next(forget_in))
                dve.tensor_scalar(neg, y, -1.0, 0.0, ALU.mult, ALU.max).then_inc(vec_done, 1)
                dve.wait_ge(vec_done, c.next(vec_done))
                dve.wait_ge(forget_out, c.next(forget_out))
                dve.tensor_tensor_scan(run, soft, neg, 0.0, ALU.add, ALU.add).then_inc(forget_in, 1)
                dve.wait_ge(forget_in, c.next(forget_in))
                dve.wait_ge(forget_out, c.next(forget_out))
                run_hi = l_rows(1).bitcast(F32)
                lo(soft, run, l_rows(1)).then_inc(vec_done, 1)
                dve.wait_ge(vec_done, c.next(vec_done))

                def mask(k):
                    return cst[:, C_MASK + k:C_MASK + k + 1]

                dve.scalar_tensor_tensor(bias_l[:], run_hi, mask(0), base_l[:], ALU.mult, ALU.add).then_inc(vec_done, 1)
                dve.wait_ge(vec_done, c.next(vec_done))
                dve.scalar_tensor_tensor(bias_l[:], soft, mask(1), bias_l[:], ALU.mult, ALU.add).then_inc(vec_done, 1)
                dve.wait_ge(vec_done, c.next(vec_done))
                dve.scalar_tensor_tensor(neg, run_hi, mask(2), base_r[:], ALU.mult, ALU.add).then_inc(vec_done, 1)
                dve.wait_ge(vec_done, c.next(vec_done))
                dve.scalar_tensor_tensor(bias_r, soft, mask(3), neg, ALU.mult, ALU.add).then_inc(vec_done, 1)
                dve.wait_ge(vec_done, c.next(vec_done))

            def stage(k, scale):
                dve.wait_ge(unit_done, c.next(unit_done))
                dve.scalar_tensor_tensor(tile(k % 2), ps[:, k % 2, :], scale, rstd[:], ALU.mult, ALU.mult
                                         ).then_inc(staged, 1)
                split(k % SLOTS)

            def stage_qk(branch, which, k):
                stage(k, SCALE if which == 0 else 1.0)
                dve.wait_ge(qk_hi_set, c.next(qk_hi_set))
                lo(qk(branch, which + 1), tile(k % 2), qk(branch, which)).then_inc(qk_set, 1)

            def rows(head, slot_):
                dve.tensor_scalar(l_rows(slot_), bias_l[:], cst[:, bass.ds(head + C_SEL, 1)], None, ALU.mult
                                  ).then_inc(rows_set, 1)

            def block_max(buf, i):
                dve.wait_ge(score_set, c.next(score_set))
                top = stat[:, 24 + i:25 + i]
                dve.reduce_max(top, ps[:, SB0 + i, 0:(i + 1) * P], AX_X).then_inc(vec_done, 1)
                dve.wait_ge(vec_done, c.next(vec_done))
                dve.tensor_scalar(neg_max(buf, i), top, -1.0, None, ALU.mult).then_inc(max_set, 1)

            def softmax(buf, done):
                for i in range(NQ + 1):
                    if i < NQ:
                        block_max(buf, i)
                    if i > 0:
                        dve.wait_ge(exp_set, c.next(exp_set))
                        dve.reciprocal(inverse(buf, i - 1), total(buf, i - 1)).then_inc(vec_done, 1)
                        dve.wait_ge(vec_done, c.next(vec_done))
                        q = query_block(buf, i - 1)
                        dve.tensor_scalar(q, q, inverse(buf, i - 1), None, ALU.mult).then_inc(done, 1)
                        c.skip(done)

            def difference(layer):
                dve.wait_ge(vec_done, c.peek(vec_done, 0))
                for i in range(NQ + 1):
                    if i < NQ:
                        block_max(1, i)
                    if i > 0:
                        dve.wait_ge(exp_set, c.next(exp_set))
                        dve.reciprocal(inverse(1, i - 1), total(1, i - 1)).then_inc(vec_done, 1)
                        dve.wait_ge(vec_done, c.next(vec_done))
                        dve.tensor_scalar(inverse(1, i - 1), inverse(1, i - 1), lam[:, bass.ds(layer, 1)],
                                          None, ALU.mult).then_inc(vec_done, 1)
                        dve.wait_ge(vec_done, c.next(vec_done))
                        dve.scalar_tensor_tensor(query_block(0, i - 1), query_block(1, i - 1), inverse(1, i - 1),
                                                 query_block(0, i - 1), ALU.mult, ALU.add).then_inc(prob_set, 1)

            def turned_lo():
                for j in range(NQ):
                    dve.wait_ge(pt_hi_set, c.next(pt_hi_set))
                    lo(keys(PT_LO, j), ps[:, SB0 + j, 0:(NQ - j) * P], keys(PT_HI, j)).then_inc(pt_set, 1)

            def stick_softplus():
                c.skip(score_set, NQ)
                for j in range(NQ):
                    dve.wait_ge(log_set, c.next(log_set))
                    k = key_block(1, j)
                    dve.scalar_tensor_tensor(k, stick_bank(j), 0.0, k, ALU.max, ALU.add).then_inc(vec_done, 1)
                    dve.wait_ge(vec_done, c.next(vec_done))
                    dve.tensor_tensor(k[:, 0:P], k[:, 0:P], strict01, ALU.mult).then_inc(sp_set, 1)
                for j in range(NQ):
                    dve.wait_ge(pt_hi_set, c.next(pt_hi_set))
                    lo(keys(PT_LO, j), key_block(1, j), keys(PT_HI, j)).then_inc(pt_set, 1)

            def stick_lo():
                for j in range(NQ):
                    dve.wait_ge(pt_hi_set, c.next(pt_hi_set))
                    lo(keys(PT_LO, j), key_block(0, j), keys(PT_HI, j)).then_inc(pt_set, 1)

            def values_lo(branch):
                if branch == 0:
                    dve.wait_ge(v_hi_set, c.next(v_hi_set))
                    lo(val(0, 0, 1), ps[:, AUX, :], val(0, 0, 0)).then_inc(v_set, 1)
                else:
                    dve.wait_ge(v_hi_set, c.next(v_hi_set, 2))
                    for hd in range(2):
                        last = lo(half_tile(val(branch, hd, 1), hd), half_tile(ps[:, AUX, :], hd),
                                  half_tile(val(branch, hd, 0), hd))
                    last.then_inc(v_set, 1)

            def output_lo(branch, t, layer):
                at = (t + branch * NT) * SEQ
                src = ps[:, OB, :]
                if branch == 0:
                    dve.wait_ge(o_rstd, c.next(o_rstd))
                    dve.scalar_tensor_tensor(tile(7), ps[:, OB, :], lam[:, bass.ds(layer + 2, 1)], tile(7),
                                             ALU.mult, ALU.mult).then_inc(o_norm, 1)
                    dve.wait_ge(o_norm, c.next(o_norm))
                    src = tile(7)
                dve.wait_ge(o_hi_set, c.next(o_hi_set))
                lo(area[:, bass.ds(at + O_LO, SEQ)], src, area[:, bass.ds(at + O_HI, SEQ)]).then_inc(o_set, 1)

            def heads(t, layer, diff_before):
                if diff_before:
                    softmax(0, vec_done)
                stage_qk(2, 0, 0)
                if diff_before:
                    difference(layer)
                stage_qk(2, 2, 1)
                if diff_before:
                    turned_lo()
                stage(2, 1.0)
                stick_softplus()
                stage_qk(1, 0, 3)
                values_lo(2)
                stick_lo()
                if diff_before:
                    output_lo(0, t - 1, layer)
                stage_qk(1, 2, 4)
                stick_softplus()
                stage(5, 1.0)
                stick_lo()
                rows(t * 2, 0)
                stage_qk(0, 0, 6)
                output_lo(2, t, layer)
                softmax(0, prob_set)
                values_lo(1)
                rows(t * 2 + 1, 1)
                stage_qk(0, 2, 7)
                turned_lo()
                stage(8, 1.0)
                softmax(1, prob_set)
                rows(t + N_FOX, 0)
                values_lo(0)
                turned_lo()
                output_lo(1, t, layer)

            def gates(units):
                for k in range(3):
                    a = tile(6 * (k % 2))
                    dve.wait_ge(unit_done, c.next(unit_done))
                    dve.tensor_tensor(a, ps[:, k, :], rstd[:], ALU.mult).then_inc(tail_read, 1)
                    split(k)
                dve.wait_ge(gate_out, c.next(gate_out, 3))

            def mix(banks, at, inside):
                m, part = tile(4), tile(5)
                for b in range(3):
                    if b in inside:
                        dve.wait_ge(proj_mm, c.next(proj_mm))
                    elif inside == (0, 2):
                        dve.wait_ge(unit_done, c.next(unit_done))
                    dve.tensor_tensor(part if b else m, tile(1 + b), ps[:, banks[b], :], ALU.mult
                                      ).then_inc(tail_read, 1)
                    dve.wait_ge(tail_read, c.next(tail_read))
                    if b:
                        done = m_mid if b == 2 else vec_done
                        dve.tensor_tensor(m, m, part, ALU.add).then_inc(done, 1)
                        dve.wait_ge(done, c.next(done))
                    if b == 1 and inside == (0, 2):
                        split(0)
                dve.wait_ge(m_hi_set, c.next(m_hi_set))
                lo(area[:, bass.ds(at + M_LO, SEQ)], m, area[:, bass.ds(at + M_HI, SEQ)]).then_inc(m_set, 1)

            def mixer(layer, gain):
                forget(layer)
                heads(0, layer, False)
                with c.turns(1, NT) as t:
                    heads(t, layer, True)
                softmax(0, vec_done)
                difference(layer)
                turned_lo()
                output_lo(0, NT - 1, layer)
                with c.turns(0, ND // 2) as i:
                    c.skip(tail_read, 3)
                    gates(0)
                    mix((3, 4, 5), i * (2 * SEQ), (0, 2))
                    for k in (1, 2):
                        dve.wait_ge(unit_done, c.next(unit_done))
                        split(k)
                    c.skip(tail_read, 3)
                    gates(6)
                    mix((6, 7, 4), i * (2 * SEQ) + SEQ, (1,))
                dve.memset(acc, 0.0).then_inc(vec_done, 1)
                dve.wait_ge(vec_done, c.next(vec_done))
                for d in range(ND):
                    dve.wait_ge(unit_done, c.next(unit_done))
                    update(d * SEQ, 6 + d % 2, 1.0, gain + d)
                    split(d % SLOTS)
                dve.wait_ge(unit_done, c.next(unit_done))
                split(2)

            dve.wait_ge(small_landed, 16 * 6)
            dve.sem_inc(up_set, 3)
            dve.sem_inc(h_set, 2)
            dve.sem_inc(o_set, 1)
            dve.sem_inc(tail_read, 12)
            c.skip(up_set, 3)
            c.skip(h_set, 2)
            c.skip(tail_read, 12)
            n = DEPTH * 2
            pairs = HG[:, 0:n * HEAD]
            dve.tensor_tensor(pairs, SQ[:, 0:n * HEAD], SQ[:, n * HEAD:2 * n * HEAD], ALU.mult).then_inc(vec_done, 1)
            dve.wait_ge(vec_done, c.next(vec_done))
            dve.reduce_sum(lam[:, 8:8 + n], pairs.rearrange("p (a b) -> p a b", b=HEAD), AX_X).then_inc(lam_in, 1)
            dve.memset(acc, 0.0).then_inc(vec_done, 1)
            dve.wait_ge(vec_done, c.next(vec_done))
            dve.memset(v_area[:].bitcast(F32), 0.0).then_inc(vec_done, 1)
            dve.wait_ge(vec_done, c.next(vec_done))
            dve.wait_ge(lam_out, 1)
            for layer in range(DEPTH):
                e = 4 + 2 * layer
                dve.tensor_tensor(lam[:, layer:layer + 1], lam[:, e + 1:e + 2], lam[:, e:e + 1], ALU.subtract).then_inc(vec_done, 1)
                dve.wait_ge(vec_done, c.next(vec_done))
                dve.tensor_scalar(lam[:, layer:layer + 1], lam[:, layer:layer + 1], -lam_init(layer), None,
                                  ALU.add).then_inc(vec_done, 1)
                dve.wait_ge(vec_done, c.next(vec_done))
                dve.tensor_scalar(lam[:, 2 + layer:3 + layer], par[:, P_SUBLN + layer:P_SUBLN + layer + 1],
                                  1.0 - lam_init(layer), None, ALU.mult).then_inc(vec_done, 1)
                dve.wait_ge(vec_done, c.next(vec_done))
            dve.tensor_copy(base_l[:], scratch[:, 1024:1024 + SEQ])
            dve.tensor_copy(base_r[:], scratch[:, 1024 + SEQ:1024 + 2 * SEQ]).then_inc(const_set, 1)
            for k in range(SLOTS):
                split(k)
            for d in range(ND):
                fresh(d * SEQ, P_GAIN + d, first=d == 0)
            with c.turns(0, DEPTH) as layer:
                ffn(layer * (3 * ND) + (P_GAIN + ND))
                mixer(layer, layer * (3 * ND) + (P_GAIN + 2 * ND))
                ffn(layer * (3 * ND) + (P_GAIN + 3 * ND))
            dve.wait_ge(rstd_set, c.next(rstd_set))
            for d in range(ND):
                if d >= 2:
                    dve.wait_ge(stored[d % 2], 16 * (d // 2))
                g = P_GAIN + 3 * DEPTH * ND + d
                dve.scalar_tensor_tensor(tile(d % 2), h[:, d * SEQ:(d + 1) * SEQ], par[:, g:g + 1], rstd[:],
                                         ALU.mult, ALU.mult).then_inc(y_set, 1)



def constants():
    k, q = np.arange(P)[:, None], np.arange(P)[None, :]
    c = np.zeros((P, C_END), np.float32)
    c[:, C_IDENT:C_IDENT + P] = k == q
    c[:, C_STRICT01:C_STRICT01 + P] = k < q
    c[:, C_ONES:C_ONES + P] = 1
    row, group = np.arange(P) % 32, np.arange(P) // 32
    for head in range(N_FOX):
        c[:, C_SEL + head] = row == head
    for head in range(N_DIFF):
        c[:, C_SEL + N_FOX + head] = (row == N_FOX) * 2.0 ** (-8.0 * (head + 1) / N_DIFF)
    for g, sign in enumerate((-1, -1, 1, 1)):
        c[:, C_MASK + g] = sign * ((group == g) & (row < N_FOX))
    c[:, C_EPS], c[:, C_EPS + 1] = EPS, SUBLN_EPS
    r = np.zeros((P, ROUNDED * P), np.float32)

    def block(n):
        return r[:, n * P:(n + 1) * P]

    block(R_IDENT)[:] = k == q
    block(R_CAUSAL)[:] = np.where(q > k, NEG, 0)
    block(R_STRICT)[:] = np.where(k >= q, NEG, 0)
    block(R_NEGTRI)[:] = np.where(k >= q, -1, 0)
    block(R_NEGONES)[:] = -1
    pos = np.arange(SEQ)
    b = np.zeros((P, 2 * SEQ), np.float32)
    left, right = b[:, :SEQ], b[:, SEQ:]
    left[(group >= 2) & (row < N_FOX)] = 1
    right[(group < 2) & (row < N_FOX)] = 1
    left[N_FOX], right[N_FOX] = -pos, 1
    left[2 * 32 + N_FOX], right[2 * 32 + N_FOX] = 1, pos
    return c, r, b


def weight_stream(a):
    empty = np.zeros((1, P, UNIT, P), np.float32)
    branch = {"a": 0, "b": 3 * 512, "c": 9 * 512 + N_FOX - 3 * 512}
    gate0 = 9 * 512 + N_FOX

    def columns(w, at, n=1):
        return w[:, at:at + n * P].reshape(ND, P, n, P).transpose(2, 1, 0, 3)

    def ffn(w1, w3, w2):
        both = np.stack([columns(w1, 0, NF), columns(w3, 0, NF)], 1).reshape(2 * NF, P, UNIT, P)
        down = w2.reshape(NF, P, ND, P).transpose(2, 1, 0, 3)
        down = np.concatenate([down, np.zeros((ND, P, W2_UNITS * UNIT - NF, P), np.float32)], 2)
        down = down.reshape(ND, P, W2_UNITS, UNIT, P).transpose(0, 2, 1, 3, 4).reshape(-1, P, UNIT, P)
        return [both, empty, down]

    parts = []
    for n in range(DEPTH):
        parts += ffn(a["ffn1_w1"][n], a["ffn1_w3"][n], a["ffn1_w2"][n])
        w_in = a["w_in"][n]
        for t in range(NT):
            for name in "cba":
                for which in range(3):
                    parts.append(columns(w_in, branch[name] + which * 512 + t * P))
        proj = np.concatenate([a[f"proj_{x}"][n].reshape(NT, P, ND, P) for x in "abc"], 0)
        for d in range(0, ND, 2):
            gates = [[columns(w_in, gate0 + b * D_MODEL + e * P) for b in range(3)] for e in (d, d + 1)]
            blocks = proj[:, :, d:d + 2].transpose(2, 0, 1, 3).reshape(3, UNIT, P, P).transpose(0, 2, 1, 3)
            parts += gates[0] + [blocks] + gates[1]
        parts += [columns(a["w_out"][n], 0, ND), empty]
        parts += ffn(a["ffn2_w1"][n], a["ffn2_w3"][n], a["ffn2_w2"][n])
    parts += [empty] * SLOTS
    return np.concatenate(parts, 0).reshape(-1, P, UNIT * P)


def small_params(a):
    p = np.zeros((P, P_END), np.float32)
    gains = []
    for n in range(DEPTH):
        gains += [a["ffn1_norm"][n], a["mix_norm"][n], a["ffn2_norm"][n]]
        p[:, P_SUBLN + n] = a["diff_subln"][n]
        p[:, P_FB + n] = np.tile(a["forget_bias"][n], P // N_FOX)
        wf = a["w_in"][n][:, 6 * 512:6 * 512 + N_FOX].reshape(ND, P, N_FOX).transpose(1, 0, 2)
        p[:, P_WF + n * ND * N_FOX:P_WF + (n + 1) * ND * N_FOX] = wf.reshape(P, -1)
    gains.append(a["final_norm"])
    p[:, P_GAIN:P_GAIN + GAINS * ND] = np.stack(gains).reshape(GAINS * ND, P).transpose(1, 0)
    return p


def lambda_rows(a):
    rows = [a[f"diff_l{x}{m}"][n] for x in "qk" for n in range(DEPTH) for m in (1, 2)]
    return np.tile(np.concatenate(rows)[None, :], (P, 1))


def kernel(**inputs):
    import concourse.bacc as bacc
    from concourse.bass_utils import run_bass_kernel_spmd

    a = {name: np.ascontiguousarray(v) for name, v in inputs.items()}
    c, r, b = constants()
    arrays = {
        "x": np.ascontiguousarray(a["x"][0].reshape(SEQ, ND, P).transpose(2, 1, 0)).reshape(P, ND * SEQ),
        "weights": weight_stream(a),
        "params": small_params(a),
        "lambdas": lambda_rows(a),
        "const": c, "const_r": r, "const_b": b,
    }
    nc = bacc.Bacc("TRN2", target_bir_lowering=False, num_devices=1, dynamic_dma_scratch_size=1024)
    aps = [nc.dram_tensor(name, v.shape, F32, kind="ExternalInput").ap() for name, v in arrays.items()]
    out = nc.dram_tensor("out", (ND, P, SEQ), F32, kind="ExternalOutput").ap()
    trunk(nc, *aps, out)
    got = run_bass_kernel_spmd(nc, [arrays], core_ids=[0]).results[0]["out"]
    return np.ascontiguousarray(got.transpose(2, 0, 1).reshape(1, SEQ, D_MODEL))
```

```python
from contextlib import ExitStack, contextmanager
import math

import numpy as np
import concourse.bass as bass
from concourse import mybir

F32 = mybir.dt.float32
F32R = mybir.dt.float32r
BF16 = mybir.dt.bfloat16
F16 = mybir.dt.float16
ACT = mybir.ActivationFunctionType
ALU = mybir.AluOpType
AX_X = mybir.AxisListType.X

P = 128
D_MODEL, SEQ, DEPTH, D_FF = 1024, 512, 2, 2816
HEAD = 64
N_DIFF, N_FOX, N_SB = 4, 8, 8
EPS, SUBLN_EPS = 1e-6, 1e-5
ND = D_MODEL // P
NF = D_FF // P
NQ = SEQ // P
NT = 4
SCALE = 1.0 / math.sqrt(HEAD)
LN_EXP = "natural_log_exp_and_others"
NEG = -1.0e30

UNIT = 8
SLOTS = 3
FFN_A_UNITS = 2 * NF + 1
W2_UNITS = 3
HEAD_UNITS = 9
TAIL_UNITS = 9
OUT_UNITS = ND + 1
LAYER_UNITS = 2 * (FFN_A_UNITS + W2_UNITS * ND) + HEAD_UNITS * NT + TAIL_UNITS * ND // 2 + OUT_UNITS
N_UNITS = DEPTH * LAYER_UNITS
assert LAYER_UNITS % SLOTS == 0 and FFN_A_UNITS % SLOTS == 0 and OUT_UNITS % SLOTS == 0

Q_OFF = [P * i * (i + 1) // 2 for i in range(NQ)]
K_OFF = [P * (j * NQ - j * (j - 1) // 2) for j in range(NQ)]
TRI = P * NQ * (NQ + 1) // 2
PT_OFF = K_OFF[:-1] + [K_OFF[-1] + P]
PT_SIZE = TRI + P
WIDE = 2 * P

V_AT = (0, 2 * SEQ, 5 * SEQ, 8 * SEQ)
V_COLS = V_AT[-1]

GAINS = 3 * DEPTH + 1
P_GAIN = 0
P_SUBLN = P_GAIN + GAINS * ND
P_FB = P_SUBLN + DEPTH
P_WF = P_FB + DEPTH
P_END = P_WF + DEPTH * ND * N_FOX
C_IDENT, C_STRICT01, C_ONES, C_SEL = 0, P, 2 * P, 3 * P
C_MASK = C_SEL + N_FOX + N_DIFF
C_EPS = C_MASK + 4
C_END = C_EPS + 2
R_IDENT, R_CAUSAL, R_STRICT, R_NEGTRI, R_NEGONES, ROUNDED = 0, 1, 2, 3, 4, 5
IN_BF16 = R_NEGTRI


TAIL_ORDER = (1, 2, 0)


def lam_init(layer):
    return 0.8 - 0.6 * math.exp(-0.3 * layer)


class Counts:

    def __init__(self, eng, sems):
        self.eng = eng
        self.reg, self.more, self.base = {}, {}, {}
        for s in sems:
            self.reg[s] = eng.alloc_register(f"count_{len(self.reg)}_{eng.engine}".replace(".", "_"))
            eng.reg_mov(self.reg[s], 0)
            self.more[s], self.base[s] = 0, 0

    def value(self, sem, ahead=0):
        if self.base[sem] is None:
            self.base[sem] = self.eng.snap(self.reg[sem])
        return self.base[sem] + (self.more[sem] + ahead)

    def skip(self, sem, n=1):
        self.more[sem] += n

    def next(self, sem, n=1):
        self.more[sem] += n
        return self.value(sem)

    def peek(self, sem, n=1):
        return self.value(sem, n)

    def fold(self):
        for s, n in self.more.items():
            if n:
                self.eng.reg_add(self.reg[s], self.reg[s], n)
            self.more[s] = 0
            self.base[s] = None

    def read(self):
        for s in self.reg:
            self.base[s] = self.eng.snap(self.reg[s])

    @contextmanager
    def turns(self, first, last):
        self.fold()
        with self.eng.Fori(first, last) as i:
            self.read()
            yield i
            self.fold()
        self.read()


def trunk(nc, x, stream, params, lambdas, const, const_r, const_b, out):
    ctx = ExitStack()
    with ctx:
        def sb(name, cols, dt=F32):
            return ctx.enter_context(nc.sbuf_tensor(name, [P, cols], dt))

        O_HI, O_LO = 0, 3 * NT * SEQ
        QK = 2 * O_LO
        PT_HI = QK + 3 * 5 * SEQ
        PT_LO = PT_HI + PT_SIZE
        L_ROWS = PT_LO + PT_SIZE
        R_ROWS = L_ROWS + 2 * SEQ
        AREA = R_ROWS + SEQ
        assert AREA >= NF * 2 * SEQ
        M_HI, M_LO = QK, QK + ND * SEQ

        h = sb("h", ND * SEQ)
        u_hi = sb("u_hi", ND * SEQ, F32R)
        u_lo = sb("u_lo", ND * SEQ, F32R)
        w_raw = sb("w_raw", SLOTS * UNIT * P)
        w_hi = sb("w_hi", SLOTS * UNIT * P, F32R)
        w_lo = sb("w_lo", SLOTS * UNIT * P, F32R)
        rstd = sb("rstd", SEQ)
        area = sb("area", AREA, F32R)
        v_area = sb("v_area", V_COLS, F32R)
        scratch = sb("scratch", 8 * SEQ)
        bias_l = sb("bias_l", SEQ)
        base_l = sb("base_l", SEQ, F16)
        base_r = sb("base_r", SEQ, F16)
        cst = sb("cst", C_END)
        cst_b = sb("cst_b", IN_BF16 * P, BF16)
        cst_r = sb("cst_r", (ROUNDED - IN_BF16) * P, F32R)
        par = sb("par", P_END)
        lam = sb("lam", 16)
        stat = sb("stat", 32)

        ident, strict01, ones = (cst[:, c:c + P] for c in (C_IDENT, C_STRICT01, C_ONES))
        ident_b, causal_b, strict_b = (cst_b[:, k * P:(k + 1) * P] for k in (R_IDENT, R_CAUSAL, R_STRICT))
        negtri_r, negones_r = (cst_r[:, (k - IN_BF16) * P:(k - IN_BF16 + 1) * P] for k in (R_NEGTRI, R_NEGONES))

        def g_hi(f):
            return area[:, f * 2 * SEQ:f * 2 * SEQ + SEQ]

        def g_lo(f):
            return area[:, f * 2 * SEQ + SEQ:(f + 1) * 2 * SEQ]

        def half(hd):
            return slice(hd * HEAD, (hd + 1) * HEAD)

        def q_twice(branch, hd):
            at = QK + (branch * 5 + hd) * SEQ
            return area[:, at:at + SEQ]

        def k_both(branch, hd):
            at = QK + (branch * 5 + 2 + hd) * SEQ
            return area[:, at:at + SEQ]

        def q_rest(branch):
            at = QK + (branch * 5 + 4) * SEQ
            return area[:, at:at + SEQ]

        bias_r = area[:, R_ROWS:R_ROWS + SEQ]

        def l_rows(slot):
            return area[:, L_ROWS + slot * SEQ:L_ROWS + (slot + 1) * SEQ]

        def val(branch, part):
            at = V_AT[branch] + part * (V_AT[branch + 1] - V_AT[branch]) // 2
            return v_area[:, at:at + (V_AT[branch + 1] - V_AT[branch]) // 2]

        def val_block(branch, head, part, j):
            at = j * P if branch == 0 else j * 3 * HEAD + head * HEAD
            return val(branch, part)[:, at:at + P]

        def tile(k):
            return scratch[:, k * SEQ:(k + 1) * SEQ]

        def first_square(d):
            return (tile(4), tile(6), bias_l[:], rstd[:])[d % 4]

        prob = [scratch[:, 2 * SEQ:2 * SEQ + TRI], scratch[:, 2 * SEQ + TRI:2 * SEQ + 2 * TRI]]
        acc = tile(7)

        ps = ctx.enter_context(nc.psum_tensor("ps", [P, 8, SEQ], F32))
        AUX, OB, SB0 = 2, 3, 4

        def slot(w, k, b=0):
            return w[:, (k * UNIT + b) * P:(k * UNIT + b + 1) * P]

        def stick_bank(j):
            spare = P if j == NQ - 1 else 0
            return ps[:, SB0 + j, spare:spare + (NQ - j) * P]

        def sem(name):
            return ctx.enter_context(nc.semaphore(name))

        x_landed = [sem(f"x_landed{k}") for k in range(2)]
        small_landed = sem("small_landed")
        const_set = sem("const_set")
        landed = [sem(f"landed{k}") for k in range(SLOTS)]
        w_hi_set = sem("w_hi_set")
        w_set = sem("w_set")
        unit_done = sem("unit_done")
        vec_done = sem("vec_done")
        act_done = sem("act_done")
        zeros_set = sem("zeros_set")
        h_set = sem("h_set")
        sq_set = sem("sq_set")
        acc_set = sem("acc_set")
        u_hi_set = sem("u_hi_set")
        u_set = sem("u_set")
        ms_set = sem("ms_set")
        rstd_set = sem("rstd_set")
        gate_in = sem("gate_in")
        gate_out = sem("gate_out")
        up_set = sem("up_set")
        hid_set = sem("hid_set")
        g_hi_set = sem("g_hi_set")
        g_set = sem("g_set")
        lam_in = sem("lam_in")
        lam_out = sem("lam_out")
        wf_hi_set = sem("wf_hi_set")
        wf_set = sem("wf_set")
        forget_mm = sem("forget_mm")
        forget_in = sem("forget_in")
        forget_out = sem("forget_out")
        staged = sem("staged")
        qk_hi_set = sem("qk_hi_set")
        qk_set = sem("qk_set")
        turned = sem("turned")
        v_hi_set = sem("v_hi_set")
        v_set = sem("v_set")
        rows_set = sem("rows_set")
        score_set = sem("score_set")
        max_set = sem("max_set")
        exp_set = sem("exp_set")
        prob_set = sem("prob_set")
        probs_turned = sem("probs_turned")
        log_set = sem("log_set")
        sp_set = sem("sp_set")
        pt_hi_set = sem("pt_hi_set")
        pt_set = sem("pt_set")
        stick_set = sem("stick_set")
        o_mm = sem("o_mm")
        o_sq = sem("o_sq")
        o_ms = sem("o_ms")
        o_rstd = sem("o_rstd")
        o_norm = sem("o_norm")
        o_hi_set = sem("o_hi_set")
        o_set = sem("o_set")
        proj_mm = sem("proj_mm")
        tail_read = sem("tail_read")
        m_mid = sem("m_mid")
        m_hi_set = sem("m_hi_set")
        m_set = sem("m_set")
        y_set = sem("y_set")
        stored = sem("stored")

        block = ctx.enter_context(nc.Block())

        @block.sync
        def _(sp):
            half = ND * SEQ // 2
            sp.dma_start(par[:], params).then_inc(x_landed[0], 16)
            sp.dma_start(cst[:], const).then_inc(x_landed[0], 16)
            sp.dma_start(h[:, 0:half], x[:, 0:half]).then_inc(x_landed[0], 16)
            counts = Counts(sp, [w_set])

            def load(unit, k):
                sp.dma_start(w_raw[:, k * UNIT * P:(k + 1) * UNIT * P], stream[unit, :, :]).then_inc(landed[k], 16)

            load(0, 0)
            sp.dma_start(h[:, half:], x[:, half:]).then_inc(x_landed[1], 16)
            load(1, 1)
            load(2, 2)
            sp.dma_start(scratch[:, 0:ROUNDED * P], const_r).then_inc(small_landed, 16)
            sp.dma_start(scratch[:, 1024:1024 + 2 * SEQ], const_b).then_inc(small_landed, 16)
            sp.dma_start(scratch[:, 5 * SEQ:6 * SEQ], lambdas).then_inc(small_landed, 16)
            with counts.turns(0, N_UNITS // SLOTS) as i:
                for k in range(SLOTS):
                    sp.wait_ge(w_set, counts.next(w_set))
                    sp.dma_start(w_raw[:, k * UNIT * P:(k + 1) * UNIT * P],
                                 stream[bass.ds(i * SLOTS + SLOTS + k, 1), :, :].rearrange("a p n -> p (a n)")
                                 ).then_inc(landed[k], 16)
            for d in range(ND):
                sp.wait_ge(y_set, d + 1)
                sp.dma_start(out[:, d * SEQ:(d + 1) * SEQ], tile(d)).then_inc(stored, 16)
            sp.wait_ge(stored, 16 * ND)
            for k in range(SLOTS):
                sp.wait_ge(landed[k], 16 * (N_UNITS // SLOTS + 1))

        @block.gpsimd
        def _(pool):
            pool.memset(v_area[:].bitcast(F32), 0.0).then_inc(zeros_set, 1)

        @block.tensor
        def _(pe):
            c = Counts(pe, [w_set, u_set, acc_set, rstd_set, up_set, g_set, h_set, wf_set, staged,
                            rows_set, qk_set, v_set, exp_set, prob_set, pt_set, o_sq, o_rstd, o_set,
                            tail_read, m_set])

            def three(dst, hi, lo, x_hi, x_lo, start, stop, **kw):
                pe.matmul(dst, hi, x_hi, start=start, stop=False, **kw)
                pe.matmul(dst, hi, x_lo, start=False, stop=False, **kw)
                return pe.matmul(dst, lo, x_hi, start=False, stop=stop, **kw)

            def u(k):
                return u_hi[:, k * SEQ:(k + 1) * SEQ], u_lo[:, k * SEQ:(k + 1) * SEQ]

            def u_unit(bank, k, part=(0, UNIT), first=False):
                if part[0] == 0:
                    pe.wait_ge(w_set, c.next(w_set))
                for b in range(*part):
                    if first:
                        pe.wait_ge(u_set, c.next(u_set))
                    last = three(ps[:, bank, :], slot(w_hi, k, b), slot(w_lo, k, b), *u(b),
                                 start=b == 0, stop=b == UNIT - 1)
                return last

            def sum_of_squares():
                pe.wait_ge(acc_set, c.next(acc_set, ND))
                pe.matmul(ps[:, 7, :], ones, acc, start=True, stop=True).then_inc(ms_set, 1)

            def ffn():
                pe.wait_ge(up_set, c.next(up_set))
                u_unit(0, 0, first=True).then_inc(unit_done, 1)
                sum_of_squares()
                u_unit(1, 1).then_inc(unit_done, 2)
                c.skip(w_set)
                with c.turns(0, NF // 3) as _i:
                    for f in range(3):
                        pe.wait_ge(up_set, c.next(up_set))
                        pair = (f + 1) % 3
                        u_unit(2 * pair, 2 * f % SLOTS).then_inc(unit_done, 1)
                        u_unit(2 * pair + 1, (2 * f + 1) % SLOTS).then_inc(unit_done, 1)
                pe.wait_ge(rstd_set, c.next(rstd_set))
                with c.turns(0, ND // 2) as _i:
                    for d in range(2):
                        pe.wait_ge(h_set, c.next(h_set))
                        for k in range(W2_UNITS):
                            pe.wait_ge(w_set, c.next(w_set))
                            for b in range(min(UNIT, NF - k * UNIT)):
                                f = k * UNIT + b
                                if f == 0:
                                    pe.wait_ge(g_set, c.peek(g_set, NF - 3))
                                elif f >= NF - 3:
                                    pe.wait_ge(g_set, c.peek(g_set, f + 1))
                                last = three(ps[:, 6 + d, :], slot(w_hi, k, b), slot(w_lo, k, b),
                                             g_hi(f), g_lo(f), start=f == 0, stop=f == NF - 1)
                            last.then_inc(unit_done, 1)
                c.skip(g_set, NF)

            def forget():
                pe.wait_ge(const_set, 2)
                pe.wait_ge(wf_set, c.next(wf_set))
                for k in range(ND):
                    at = PT_HI + k * P
                    last = three(ps[:, AUX, :], area[:, at:at + P], area[:, at + ND * P:at + ND * P + P], *u(k),
                                 start=k == 0, stop=k == ND - 1)
                last.then_inc(forget_mm, 1)
                pe.wait_ge(rstd_set, c.next(rstd_set))

            def scores(branch, hd, rows):
                a, q, k = half(hd), q_twice(branch, hd), k_both(branch, hd)
                for i in range(NQ):
                    n, m = max(WIDE, (i + 1) * P), slice(i * P, (i + 1) * P)
                    dst = ps[:, SB0 + i, 0:n]
                    pe.matmul(dst, q[:, m], k[:, 0:n], start=True, stop=False)
                    pe.matmul(dst, q_rest(branch)[a, m], k[a, 0:n], start=False, stop=False)
                    pe.matmul(dst, l_rows(rows)[:, m], bias_r[:, 0:n], start=False, stop=False)
                    pe.matmul(ps[:, SB0 + i, m], ident_b, causal_b, start=False, stop=True).then_inc(score_set, 1)

            def turn_probs(buf):
                for i in range(NQ):
                    pe.wait_ge(prob_set, c.next(prob_set))
                    for j in range(i + 1):
                        at = Q_OFF[i] + j * P
                        last = pe.transpose(ps[:, SB0 + j, (i - j) * P:(i - j + 1) * P], prob[buf][:, at:at + P], ident)
                last.then_inc(probs_turned, 1)

            def turn_values(st):
                for j in range(NQ):
                    last = pe.transpose(ps[:, AUX, j * P:(j + 1) * P], tile(st)[:, j * P:(j + 1) * P], ident)
                last.then_inc(turned, 1)

            def wide_keys(j):
                n = max(WIDE, (NQ - j) * P)
                end = PT_OFF[j] + (NQ - j) * P
                return n, area[:, PT_HI + end - n:PT_HI + end], area[:, PT_LO + end - n:PT_LO + end]

            def weighted(branch, head, first, final):
                if first:
                    pe.wait_ge(v_set, c.next(v_set))
                    pe.wait_ge(o_set, c.next(o_set))
                for j in range(NQ):
                    pe.wait_ge(pt_set, c.next(pt_set))
                    v_hi, v_lo = (val_block(branch, head, p, j) for p in range(2))
                    n, w_hi_j, w_lo_j = wide_keys(j)
                    last = three(ps[:, OB, SEQ - n:SEQ], v_hi, v_lo, w_hi_j, w_lo_j,
                                 start=first and j == 0, stop=final and j == NQ - 1)
                if final:
                    last.then_inc(o_mm, 1)

            def stick_scores(hd):
                a, q, k = half(hd), q_twice(2, hd), k_both(2, hd)
                for j in range(NQ):
                    m, n = slice(j * P, (j + 1) * P), max(WIDE, (NQ - j) * P)
                    dst = ps[:, SB0 + j, 0:n]
                    pe.matmul(dst, k[:, m], q[:, SEQ - n:], start=True, stop=False)
                    pe.matmul(dst, k[a, m], q_rest(2)[a, SEQ - n:], start=False, stop=True).then_inc(score_set, 1)

            def stick_sums():
                for i in range(NQ):
                    pe.wait_ge(pt_set, c.next(pt_set))
                    n, *parts = wide_keys(i)
                    pe.matmul(stick_bank(i)[:, 0:P], ident_b, strict_b, start=False, stop=False,
                              skip_group_check=True)
                    for j in range(i + 1):
                        width = max(WIDE, (NQ - j) * P)
                        for part in parts:
                            last = pe.matmul(ps[:, SB0 + j, width - n:width], negtri_r if i == j else negones_r,
                                             part, start=False, stop=i == NQ - 1, skip_group_check=True)
                        if i == NQ - 1:
                            last.then_inc(stick_set, 1)

            def diff_norm(bank=AUX):
                pe.wait_ge(o_sq, c.next(o_sq))
                pe.matmul(ps[:, bank, :], ones, tile(7), start=True, stop=True).then_inc(o_ms, 1)

            def unit(k, first_block=0, end=UNIT, first=False):
                last = u_unit(k % 2, k % SLOTS, (first_block, end), first)
                if end == UNIT:
                    last.then_inc(unit_done, 1)

            def rest_of_tile(unit):
                pe.wait_ge(staged, c.next(staged, 2))
                unit(0, 0, 3)
                turn_values(0)
                unit(0, 3, 6)
                turn_probs(1)
                unit(0, 6)
                unit(1, 0, 1)
                weighted(1, 1, False, True)
                pe.wait_ge(rows_set, c.next(rows_set))
                pe.wait_ge(qk_set, c.next(qk_set, 2))
                scores(0, 0, 0)
                unit(1, 1, 7)
                pe.wait_ge(exp_set, c.next(exp_set, NQ))
                scores(0, 1, 0)
                c.skip(exp_set, NQ)
                unit(1, 7)

            def heads(before):
                if before:
                    rest_of_tile(unit)
                    pe.wait_ge(staged, c.next(staged))
                    unit(2)
                    turn_probs(0)
                else:
                    unit(0, first=True)
                    sum_of_squares()
                    forget()
                    unit(1)
                    pe.wait_ge(staged, c.next(staged))
                    unit(2)
                pe.wait_ge(staged, c.next(staged))
                unit(3, 0, 3)
                if before:
                    weighted(0, 0, True, True)
                unit(3, 3, 5)
                if before:
                    diff_norm()
                pe.wait_ge(qk_set, c.next(qk_set, 2))
                stick_scores(0)
                unit(3, 5)
                pe.wait_ge(staged, c.next(staged))
                unit(4, 0, 6)
                if before:
                    pe.wait_ge(o_rstd, c.next(o_rstd))
                turn_values(0)
                stick_sums()
                unit(4, 6)
                pe.wait_ge(staged, c.next(staged))
                unit(5, 0, 3)
                weighted(2, 0, True, False)
                stick_scores(1)
                unit(5, 3)
                pe.wait_ge(staged, c.next(staged))
                unit(6, 0, 7)
                stick_sums()
                unit(6, 7)
                pe.wait_ge(staged, c.next(staged))
                unit(7, 0, 4)
                weighted(2, 1, False, True)
                pe.wait_ge(rows_set, c.next(rows_set))
                pe.wait_ge(qk_set, c.next(qk_set, 2))
                scores(1, 0, 0)
                turn_values(1)
                unit(7, 4)
                pe.wait_ge(staged, c.next(staged))
                unit(8, 0, 2)
                turn_probs(0)
                unit(8, 2)
                weighted(1, 0, True, False)
                pe.wait_ge(rows_set, c.next(rows_set))
                scores(1, 1, 1)
                c.skip(exp_set, 2 * NQ)

            def mixer():
                heads(False)
                with c.turns(1, NT) as _t:
                    heads(True)

                def gate(k, first_block=0, end=UNIT):
                    last = u_unit(k, k, (first_block, end))
                    if end == UNIT:
                        last.then_inc(unit_done, 1)

                rest_of_tile(gate)
                pe.wait_ge(v_set, c.peek(v_set))
                gate(2, 0, 5)
                turn_probs(0)
                gate(2, 5, 7)
                weighted(0, 0, True, True)
                gate(2, 7)
                diff_norm(SB0)
                c.skip(o_rstd)
                tail()

            def branch_products(k0, b0, banks, waits):
                for n, branch in enumerate(TAIL_ORDER):
                    if branch == 0:
                        pe.wait_ge(o_set, c.peek(o_set))
                    pe.wait_ge(tail_read, c.peek(tail_read, waits[n]))
                    for k in range(NT):
                        b = b0 + n * NT + k
                        s, b = (k0 + b // UNIT) % SLOTS, b % UNIT
                        if b == 0:
                            pe.wait_ge(w_set, c.next(w_set))
                        at = (branch * NT + k) * SEQ
                        last = three(ps[:, banks[n], :], slot(w_hi, s, b), slot(w_lo, s, b),
                                     area[:, O_HI + at:O_HI + at + SEQ], area[:, O_LO + at:O_LO + at + SEQ],
                                     start=k == 0, stop=k == NT - 1)
                        if b == UNIT - 1 or k == NT - 1:
                            last.then_inc(unit_done if b == UNIT - 1 else proj_mm, 1)

            def tail():
                def products():
                    branch_products(0, 0, (5, 6, 3), (9, 2, 3))
                    branch_products(1, 4, (7, 4, 5), (7, 12, 12 + 1))

                def gates(before):
                    for k in range(3):
                        pe.wait_ge(tail_read, c.peek(tail_read, before + k))
                        u_unit(k, k).then_inc(unit_done, 1)

                with c.turns(0, ND // 2 - 1) as _i:
                    products()
                    gates(10)
                    gates(12 + 4)
                    c.skip(tail_read, 12)
                products()
                gates(10)
                c.skip(tail_read, 12)
                def out_blocks(d, blocks):
                    for b in blocks:
                        if d == 0:
                            pe.wait_ge(m_set, c.next(m_set))
                        last = three(ps[:, 6 + d % 2, :], slot(w_hi, d % SLOTS, b), slot(w_lo, d % SLOTS, b),
                                     area[:, M_HI + b * SEQ:M_HI + (b + 1) * SEQ],
                                     area[:, M_LO + b * SEQ:M_LO + (b + 1) * SEQ], start=b == 0, stop=b == UNIT - 1)
                    return last

                for d in range(2):
                    pe.wait_ge(h_set, c.next(h_set))
                    pe.wait_ge(tail_read, c.peek(tail_read, (2, 7)[d]))
                    pe.wait_ge(w_set, c.next(w_set))
                    out_blocks(d, range(UNIT - 1))
                for d in range(2):
                    out_blocks(d, (UNIT - 1,)).then_inc(unit_done, 1)
                for d in range(2, ND):
                    pe.wait_ge(h_set, c.next(h_set))
                    pe.wait_ge(w_set, c.next(w_set))
                    out_blocks(d, range(UNIT)).then_inc(unit_done, 1 if d < ND - 1 else 2)
                c.skip(w_set)

            with c.turns(0, DEPTH) as _l:
                ffn()
                mixer()
                ffn()
            sum_of_squares()

        SQ = tile(5)

        def times(gain):
            return par[:, bass.ds(gain, 1)]

        wf_bank = area[:, PT_HI:PT_HI + 2 * ND * P]

        def neg_max(buf, i):
            return stat[:, 4 * buf + i:4 * buf + i + 1]

        def total(buf, i):
            return stat[:, 8 + 4 * buf + i:9 + 4 * buf + i]

        def inverse(buf, i):
            return stat[:, 16 + 4 * buf + i:17 + 4 * buf + i]

        def wf_source(layer, k):
            at = P_WF + layer * (ND * N_FOX) + k * N_FOX
            return par[:, bass.ds(at, N_FOX)].unsqueeze(1).broadcast_to([P, P // N_FOX, N_FOX])

        def keys(part, j):
            return area[:, part + PT_OFF[j]:part + PT_OFF[j] + (NQ - j) * P]

        def key_block(buf, j):
            return prob[buf][:, K_OFF[j]:K_OFF[j] + (NQ - j) * P]

        def query_block(buf, i):
            return prob[buf][:, Q_OFF[i]:Q_OFF[i] + (i + 1) * P]

        def half_tile(hd):
            return ps[:, AUX, :].rearrange("p (j e) -> p j e", j=NQ)[:, :, hd * HEAD:(hd + 1) * HEAD]

        def half_val(branch, hd, part):
            at = 2 * hd * HEAD
            return val(branch, part).rearrange("p (j e) -> p j e", j=NQ)[:, :, at:at + HEAD]

        @block.scalar
        def _(act):
            c = Counts(act, [*landed, unit_done, act_done, h_set, ms_set, gate_in, hid_set, forget_in,
                             staged, turned, score_set, max_set, probs_turned, sp_set, stick_set, o_mm, o_ms,
                             o_norm, tail_read, m_mid])

            def hi(dst, src):
                return act.activation(dst, src, ACT.Copy)

            def split(k, after=True):
                if after:
                    act.wait_ge(unit_done, c.next(unit_done))
                act.wait_ge(landed[k], c.next(landed[k], 16))
                hi(w_hi[:, k * UNIT * P:(k + 1) * UNIT * P], w_raw[:, k * UNIT * P:(k + 1) * UNIT * P]
                   ).then_inc(w_hi_set, 1)

            def u_part(at, gain):
                act.activation(u_hi[:, bass.ds(at, SEQ)], h[:, bass.ds(at, SEQ)], ACT.Copy, scale=times(gain)
                               ).then_inc(u_hi_set, 1)

            def follow(at, gain):
                act.wait_ge(h_set, c.next(h_set))
                u_part(at, gain)
                act.activation(SQ, h[:, bass.ds(at, SEQ)], ACT.Square).then_inc(sq_set, 1)

            def norm():
                act.preload_act_table_set(LN_EXP)
                act.wait_ge(ms_set, c.next(ms_set))
                act.activation(rstd[:], ps[:, 7, :], ACT.Ln, bias=cst[:, C_EPS:C_EPS + 1],
                               scale=1.0 / D_MODEL).then_inc(act_done, 1)
                act.wait_ge(act_done, c.next(act_done))
                act.activation(rstd[:], rstd[:], ACT.Exp, scale=-0.5).then_inc(rstd_set, 1)

            def hidden(at, k0, k1):
                split(k0)
                act.wait_ge(gate_in, c.next(gate_in))
                act.activation(tile(2), tile(0), ACT.Silu).then_inc(gate_out, 1)
                split(k1)
                act.wait_ge(hid_set, c.next(hid_set))
                hi(area[:, bass.ds(at, SEQ)], tile(3)).then_inc(g_hi_set, 1)

            def ffn(gain):
                norm()
                act.preload_act_table(ACT.Silu)
                hidden(0, 0, 1)
                split(2)
                with c.turns(0, NF // 3) as i:
                    for f in range(3):
                        hidden(i * (6 * SEQ) + (f + 1) * (2 * SEQ), 2 * f % SLOTS, (2 * f + 1) % SLOTS)
                with c.turns(0, ND // 2) as i:
                    for d in range(2):
                        for k in range(W2_UNITS):
                            split(k)
                        follow((i * 2 + d) * SEQ, gain + (i * 2 + d))

            def forget(layer):
                for k in range(ND):
                    dst = wf_bank[:, k * P:(k + 1) * P].rearrange("p (r n) -> p r n", n=N_FOX)
                    last = hi(dst, wf_source(layer, k))
                last.then_inc(wf_hi_set, 1)
                norm()
                split_qk(2, 0, 0)
                act.wait_ge(forget_in, c.next(forget_in))
                act.activation(tile(2), tile(3), ACT.Abs).then_inc(act_done, 1)
                act.wait_ge(act_done, c.next(act_done))
                act.activation(tile(2), tile(2), ACT.Exp, scale=-1.0).then_inc(act_done, 1)
                act.wait_ge(act_done, c.next(act_done))
                act.activation(tile(2), tile(2), ACT.Ln, bias=1.0).then_inc(forget_out, 1)
                act.wait_ge(forget_in, c.next(forget_in))
                hi(l_rows(1), tile(4)).then_inc(forget_out, 1)

            def split_qk(branch, which, k):
                split(k % SLOTS)
                qk_hi(branch, which, k)

            def qk_hi(branch, which, k):
                act.wait_ge(staged, c.next(staged))
                for hd in range(2):
                    src = tile(k % 2)[half(hd), :]
                    if which == 0:
                        hi(q_twice(branch, hd)[half(1 - hd), :], src)
                        last = hi(q_twice(branch, hd)[half(hd), :], src)
                    else:
                        last = hi(k_both(branch, hd)[half(hd), :], src)
                last.then_inc(qk_hi_set, 1)

            def exps(buf):
                for i in range(NQ):
                    act.wait_ge(max_set, c.next(max_set))
                    act.activation(query_block(buf, i), ps[:, SB0 + i, 0:(i + 1) * P], ACT.Exp,
                                   bias=neg_max(buf, i), accum_out=total(buf, i)).then_inc(exp_set, 1)

            def turned_hi():
                act.wait_ge(probs_turned, c.next(probs_turned))
                for j in range(NQ):
                    hi(keys(PT_HI, j), ps[:, SB0 + j, 0:(NQ - j) * P]).then_inc(pt_hi_set, 1)

            def stick_logs():
                for step in range(NQ + 2):
                    if step < NQ:
                        act.wait_ge(score_set, c.next(score_set))
                        act.activation(key_block(0, step), stick_bank(step), ACT.Abs).then_inc(act_done, 1)
                    if 0 <= step - 1 < NQ:
                        act.wait_ge(act_done, c.next(act_done))
                        k = key_block(0, step - 1)
                        act.activation(k, k, ACT.Exp, scale=-1.0).then_inc(act_done, 1)
                    if 0 <= step - 2 < NQ:
                        act.wait_ge(act_done, c.next(act_done))
                        act.activation(key_block(1, step - 2), key_block(0, step - 2), ACT.Ln, bias=1.0
                                       ).then_inc(log_set, 1)

            def softplus_hi():
                for j in range(NQ):
                    act.wait_ge(sp_set, c.next(sp_set))
                    hi(keys(PT_HI, j), key_block(1, j)).then_inc(pt_hi_set, 1)

            def stick_weights():
                for j in range(NQ):
                    act.wait_ge(stick_set, c.next(stick_set))
                    act.activation(key_block(0, j), stick_bank(j), ACT.Exp).then_inc(act_done, 1)
                for j in range(NQ):
                    act.wait_ge(act_done, c.next(act_done))
                    hi(keys(PT_HI, j), key_block(0, j)).then_inc(pt_hi_set, 1)

            def values_hi(branch):
                act.wait_ge(turned, c.next(turned))
                if branch == 0:
                    hi(val(0, 0), ps[:, AUX, :]).then_inc(v_hi_set, 1)
                else:
                    for hd in range(2):
                        hi(half_val(branch, hd, 0), half_tile(hd)).then_inc(v_hi_set, 1)

            def output_hi(branch, t):
                at = (t + branch * NT) * SEQ + O_HI
                if branch == 0:
                    act.wait_ge(o_norm, c.next(o_norm))
                    hi(area[:, bass.ds(at, SEQ)], tile(7)).then_inc(o_hi_set, 1)
                else:
                    act.wait_ge(o_mm, c.next(o_mm))
                    hi(area[:, bass.ds(at, SEQ)], ps[:, OB, :]).then_inc(o_hi_set, 1)

            def output_square():
                act.wait_ge(o_mm, c.next(o_mm))
                act.activation(tile(7), ps[:, OB, :], ACT.Square).then_inc(o_sq, 1)

            def output_rstd(bank=AUX):
                act.wait_ge(o_ms, c.next(o_ms))
                act.activation(tile(7), ps[:, bank, :], ACT.Ln, bias=cst[:, C_EPS + 1:C_EPS + 2],
                               scale=1.0 / (2 * HEAD)).then_inc(act_done, 1)
                act.wait_ge(act_done, c.next(act_done))
                act.activation(tile(7), tile(7), ACT.Exp, scale=-0.5).then_inc(o_rstd, 1)

            def rest_of_tile(t, project):
                values_hi(0)
                turned_hi()
                split(0)
                c.skip(score_set, NQ)
                exps(0)
                output_hi(1, t - 1)
                c.skip(score_set, NQ)
                exps(1)
                split(1)
                if project:
                    qk_hi(2, 0, 0)
                turned_hi()

            def heads(t, before):
                if before:
                    rest_of_tile(t, project=True)
                    qk_hi(2, 2, 1)
                else:
                    split_qk(2, 2, 1)
                c.skip(staged)
                if before:
                    output_square()
                split(2)
                if before:
                    output_rstd()
                stick_logs()
                softplus_hi()
                if before:
                    output_hi(0, t - 1)
                split(0)
                values_hi(2)
                stick_weights()
                split(1)
                qk_hi(1, 0, 3)
                stick_logs()
                softplus_hi()
                qk_hi(1, 2, 4)
                c.skip(staged)
                split(2)
                stick_weights()
                split(0)
                c.skip(score_set, NQ)
                exps(0)
                output_hi(2, t)
                values_hi(1)
                split(1)
                turned_hi()
                qk_hi(0, 0, 6)
                qk_hi(0, 2, 7)
                c.skip(staged)
                split(2)
                c.skip(score_set, NQ)
                exps(1)

            def mixer(layer, gain):
                forget(layer)
                heads(0, False)
                with c.turns(1, NT) as t:
                    heads(t, True)
                rest_of_tile(NT, project=False)
                output_square()
                split(2)
                output_rstd(SB0)
                output_hi(0, NT - 1)

                def gates(splits=True):
                    for k in range(3):
                        if splits:
                            split(k)
                        act.wait_ge(tail_read, c.next(tail_read))
                        act.activation(tile(1 + k), tile(6 * (k % 2)), ACT.Sigmoid).then_inc(gate_out, 1)

                def mixed_hi(at):
                    c.skip(tail_read, 3)
                    act.wait_ge(m_mid, c.next(m_mid))
                    hi(area[:, bass.ds(at, SEQ)], tile(4)).then_inc(m_hi_set, 1)

                def pair(at):
                    split(0)
                    mixed_hi(at + M_HI)
                    split(1)
                    split(2)
                    gates()
                    mixed_hi(at + (M_HI + SEQ))

                act.preload_act_table(ACT.Sigmoid)
                gates(splits=False)
                with c.turns(0, ND // 2 - 1) as i:
                    pair(i * (2 * SEQ))
                    gates()
                pair((ND - 2) * SEQ)
                for d in range(ND):
                    split(d % SLOTS)
                    follow(d * SEQ, gain + d)
                split(2)

            c.skip(h_set, 2)
            c.skip(tail_read, 9)
            for k in range(2):
                act.wait_ge(x_landed[k], 16 * (3 - 2 * k))
                for d in range(k * ND // 2, (k + 1) * ND // 2):
                    u_part(d * SEQ, P_GAIN + d)
                    if d % (ND // 2) == 1:
                        split(k, after=False)
            for d in range(ND):
                if d >= 4:
                    act.wait_ge(acc_set, d - 3)
                act.activation(first_square(d), h[:, d * SEQ:(d + 1) * SEQ], ACT.Square).then_inc(sq_set, 1)
            split(2, after=False)
            act.wait_ge(small_landed, 16 * 3)
            hi(cst_b[:], scratch[:, 0:IN_BF16 * P])
            hi(cst_r[:], scratch[:, IN_BF16 * P:ROUNDED * P]).then_inc(const_set, 1)
            act.wait_ge(lam_in, 1)
            act.activation(lam[:, 4:8], lam[:, 8:12], ACT.Exp).then_inc(lam_out, 1)
            act.wait_ge(zeros_set, 1)
            with c.turns(0, DEPTH) as layer:
                ffn(layer * (3 * ND) + (P_GAIN + ND))
                mixer(layer, layer * (3 * ND) + (P_GAIN + 2 * ND))
                ffn(layer * (3 * ND) + (P_GAIN + 3 * ND))
            norm()

        @block.vector
        def _(dve):
            c = Counts(dve, [w_hi_set, unit_done, vec_done, h_set, sq_set, acc_set, u_hi_set, rstd_set, gate_out,
                             gate_in, up_set, g_hi_set, wf_hi_set, forget_mm, forget_in, forget_out, qk_hi_set,
                             v_hi_set, score_set, exp_set, log_set, pt_hi_set, o_rstd, o_norm, o_hi_set,
                             proj_mm, tail_read, m_mid, m_hi_set, prob_set, qk_set])

            def lo(dst, src, hi_part):
                return dve.tensor_tensor(dst, src, hi_part.bitcast(F32), ALU.subtract)

            def split(k):
                dve.wait_ge(w_hi_set, c.next(w_hi_set))
                at = slice(k * UNIT * P, (k + 1) * UNIT * P)
                lo(w_lo[:, at], w_raw[:, at], w_hi[:, at]).then_inc(w_set, 1)

            def u_part(at, gain):
                dve.wait_ge(u_hi_set, c.next(u_hi_set))
                dve.scalar_tensor_tensor(u_lo[:, bass.ds(at, SEQ)], h[:, bass.ds(at, SEQ)], times(gain),
                                         u_hi[:, bass.ds(at, SEQ)].bitcast(F32), ALU.mult, ALU.subtract
                                         ).then_inc(u_set, 1)

            def add_square(square):
                dve.wait_ge(sq_set, c.next(sq_set))
                dve.tensor_tensor(acc, acc, square, ALU.add).then_inc(acc_set, 1)
                dve.wait_ge(acc_set, c.next(acc_set))

            def update(at, bank, factor, gain):
                dve.scalar_tensor_tensor(h[:, bass.ds(at, SEQ)], ps[:, bank, :], factor,
                                         h[:, bass.ds(at, SEQ)], ALU.mult, ALU.add).then_inc(h_set, 1)
                dve.wait_ge(h_set, c.next(h_set))
                u_part(at, gain)
                add_square(SQ)

            def hidden(at, pair, k0, k1):
                a, b, e, v = tile(0), tile(1), tile(2), tile(3)
                dve.wait_ge(unit_done, c.next(unit_done))
                dve.tensor_tensor(a, ps[:, 2 * pair, :], rstd[:], ALU.mult).then_inc(gate_in, 1)
                c.skip(gate_in)
                split(k0)
                dve.wait_ge(unit_done, c.next(unit_done))
                dve.tensor_tensor(b, ps[:, 2 * pair + 1, :], rstd[:], ALU.mult).then_inc(up_set, 1)
                dve.wait_ge(up_set, c.next(up_set))
                dve.wait_ge(gate_out, c.next(gate_out))
                dve.tensor_tensor(v, e, b, ALU.mult).then_inc(hid_set, 1)
                split(k1)
                dve.wait_ge(g_hi_set, c.next(g_hi_set))
                lo(area[:, bass.ds(at + SEQ, SEQ)], v, area[:, bass.ds(at, SEQ)]).then_inc(g_set, 1)

            def ffn(gain):
                dve.wait_ge(rstd_set, c.next(rstd_set))
                hidden(0, 0, 0, 1)
                dve.wait_ge(unit_done, c.next(unit_done))
                split(2)
                with c.turns(0, NF // 3) as i:
                    for f in range(3):
                        hidden(i * (6 * SEQ) + (f + 1) * (2 * SEQ), (f + 1) % 3, 2 * f % SLOTS, (2 * f + 1) % SLOTS)
                dve.memset(acc, 0.0).then_inc(vec_done, 1)
                dve.wait_ge(vec_done, c.next(vec_done))
                with c.turns(0, ND // 2) as i:
                    for d in range(2):
                        for k in range(W2_UNITS - 1):
                            dve.wait_ge(unit_done, c.next(unit_done))
                            split(k)
                        dve.wait_ge(unit_done, c.next(unit_done))
                        update((i * 2 + d) * SEQ, 6 + d, 0.5, gain + (i * 2 + d))
                        split(2)

            def forget(layer):
                dve.wait_ge(wf_hi_set, c.next(wf_hi_set))
                for k in range(ND):
                    dst, hi_part = (wf_bank[:, (n + k) * P:(n + k + 1) * P].rearrange("p (r n) -> p r n", n=N_FOX)
                                    for n in (ND, 0))
                    last = lo(dst, wf_source(layer, k), hi_part)
                last.then_inc(wf_set, 1)
                dve.wait_ge(rstd_set, c.next(rstd_set))
                stage_qk(2, 0, 0)
                y, soft, neg, run = tile(3), tile(2), tile(6), tile(4)
                dve.wait_ge(forget_mm, c.next(forget_mm))
                for part in (PT_HI, PT_LO):
                    zeros = area[:, part + PT_OFF[-1] - P:part + PT_OFF[-1]]
                    dve.memset(zeros.bitcast(F32), 0.0)
                dve.tensor_tensor(y, ps[:, AUX, :], rstd[:], ALU.mult).then_inc(vec_done, 1)
                dve.wait_ge(vec_done, c.next(vec_done))
                dve.tensor_scalar(y, y, par[:, bass.ds(layer + P_FB, 1)], None, ALU.add).then_inc(forget_in, 1)
                dve.wait_ge(forget_in, c.next(forget_in))
                dve.tensor_scalar(neg, y, -1.0, 0.0, ALU.mult, ALU.max).then_inc(vec_done, 1)
                dve.wait_ge(vec_done, c.next(vec_done))
                dve.wait_ge(forget_out, c.next(forget_out))
                dve.tensor_tensor_scan(run, soft, neg, 0.0, ALU.add, ALU.add).then_inc(forget_in, 1)
                dve.wait_ge(forget_in, c.next(forget_in))
                dve.wait_ge(forget_out, c.next(forget_out))
                run_hi = l_rows(1).bitcast(F32)
                lo(soft, run, l_rows(1)).then_inc(vec_done, 1)
                dve.wait_ge(vec_done, c.next(vec_done))

                def mask(k):
                    return cst[:, C_MASK + k:C_MASK + k + 1]

                dve.scalar_tensor_tensor(bias_l[:], run_hi, mask(0), base_l[:], ALU.mult, ALU.add).then_inc(vec_done, 1)
                dve.wait_ge(vec_done, c.next(vec_done))
                dve.scalar_tensor_tensor(bias_l[:], soft, mask(1), bias_l[:], ALU.mult, ALU.add).then_inc(vec_done, 1)
                dve.wait_ge(vec_done, c.next(vec_done))
                dve.scalar_tensor_tensor(neg, run_hi, mask(2), base_r[:], ALU.mult, ALU.add).then_inc(vec_done, 1)
                dve.wait_ge(vec_done, c.next(vec_done))
                dve.scalar_tensor_tensor(bias_r, soft, mask(3), neg, ALU.mult, ALU.add).then_inc(vec_done, 1)
                dve.wait_ge(vec_done, c.next(vec_done))

            def stage(k, scale):
                if k >= 2:
                    dve.wait_ge(qk_set, c.peek(qk_set, 0))
                dve.wait_ge(unit_done, c.next(unit_done))
                dve.scalar_tensor_tensor(tile(k % 2), ps[:, k % 2, :], scale, rstd[:], ALU.mult, ALU.mult
                                         ).then_inc(staged, 1)
                split(k % SLOTS)

            def stage_qk(branch, which, k):
                stage(k, SCALE if which == 0 else 1.0)
                qk_lo(branch, which, k)

            def qk_lo(branch, which, k):
                dve.wait_ge(qk_hi_set, c.next(qk_hi_set))
                for hd in range(2):
                    src = tile(k % 2)[half(hd), :]
                    if which == 0:
                        last = lo(q_rest(branch)[half(hd), :], src, q_twice(branch, hd)[half(hd), :])
                    else:
                        last = lo(k_both(branch, hd)[half(1 - hd), :], src, k_both(branch, hd)[half(hd), :])
                last.then_inc(qk_set, 1)
                c.skip(qk_set)

            def rows(head, slot_):
                dve.tensor_scalar(l_rows(slot_), bias_l[:], cst[:, bass.ds(head + C_SEL, 1)], None, ALU.mult
                                  ).then_inc(rows_set, 1)

            def block_max(buf, i):
                dve.wait_ge(score_set, c.next(score_set))
                top = stat[:, 24 + i:25 + i]
                dve.reduce_max(top, ps[:, SB0 + i, 0:(i + 1) * P], AX_X).then_inc(vec_done, 1)
                dve.wait_ge(vec_done, c.next(vec_done))
                dve.tensor_scalar(neg_max(buf, i), top, -1.0, None, ALU.mult).then_inc(max_set, 1)

            def softmax(buf, done):
                for i in range(NQ + 1):
                    if i < NQ:
                        block_max(buf, i)
                    if i > 0:
                        dve.wait_ge(exp_set, c.next(exp_set))
                        dve.reciprocal(inverse(buf, i - 1), total(buf, i - 1)).then_inc(vec_done, 1)
                        dve.wait_ge(vec_done, c.next(vec_done))
                        q = query_block(buf, i - 1)
                        dve.tensor_scalar(q, q, inverse(buf, i - 1), None, ALU.mult).then_inc(done, 1)
                        c.skip(done)

            def difference(layer):
                dve.wait_ge(vec_done, c.peek(vec_done, 0))
                for i in range(NQ + 1):
                    if i < NQ:
                        block_max(1, i)
                    if i > 0:
                        dve.wait_ge(exp_set, c.next(exp_set))
                        dve.reciprocal(inverse(1, i - 1), total(1, i - 1)).then_inc(vec_done, 1)
                        dve.wait_ge(vec_done, c.next(vec_done))
                        dve.tensor_scalar(inverse(1, i - 1), inverse(1, i - 1), lam[:, bass.ds(layer, 1)],
                                          None, ALU.mult).then_inc(vec_done, 1)
                        dve.wait_ge(vec_done, c.next(vec_done))
                        dve.scalar_tensor_tensor(query_block(0, i - 1), query_block(1, i - 1), inverse(1, i - 1),
                                                 query_block(0, i - 1), ALU.mult, ALU.add).then_inc(prob_set, 1)

            def turned_lo():
                for j in range(NQ):
                    dve.wait_ge(pt_hi_set, c.next(pt_hi_set))
                    lo(keys(PT_LO, j), ps[:, SB0 + j, 0:(NQ - j) * P], keys(PT_HI, j)).then_inc(pt_set, 1)

            def stick_softplus():
                c.skip(score_set, NQ)
                for j in range(NQ):
                    dve.wait_ge(log_set, c.next(log_set))
                    k = key_block(1, j)
                    dve.scalar_tensor_tensor(k, stick_bank(j), 0.0, k, ALU.max, ALU.add).then_inc(vec_done, 1)
                    dve.wait_ge(vec_done, c.next(vec_done))
                    dve.tensor_tensor(k[:, 0:P], k[:, 0:P], strict01, ALU.mult).then_inc(sp_set, 1)
                for j in range(NQ):
                    dve.wait_ge(pt_hi_set, c.next(pt_hi_set))
                    lo(keys(PT_LO, j), key_block(1, j), keys(PT_HI, j)).then_inc(pt_set, 1)

            def stick_lo():
                for j in range(NQ):
                    dve.wait_ge(pt_hi_set, c.next(pt_hi_set))
                    lo(keys(PT_LO, j), key_block(0, j), keys(PT_HI, j)).then_inc(pt_set, 1)

            def values_lo(branch):
                if branch == 0:
                    dve.wait_ge(v_hi_set, c.next(v_hi_set))
                    lo(val(0, 1), ps[:, AUX, :], val(0, 0)).then_inc(v_set, 1)
                else:
                    dve.wait_ge(v_hi_set, c.next(v_hi_set, 2))
                    for hd in range(2):
                        last = lo(half_val(branch, hd, 1), half_tile(hd), half_val(branch, hd, 0))
                    last.then_inc(v_set, 1)

            def output_lo(branch, t, layer):
                at = (t + branch * NT) * SEQ
                src = ps[:, OB, :]
                if branch == 0:
                    dve.wait_ge(o_rstd, c.next(o_rstd))
                    dve.scalar_tensor_tensor(tile(7), ps[:, OB, :], lam[:, bass.ds(layer + 2, 1)], tile(7),
                                             ALU.mult, ALU.mult).then_inc(o_norm, 1)
                    dve.wait_ge(o_norm, c.next(o_norm))
                    src = tile(7)
                dve.wait_ge(o_hi_set, c.next(o_hi_set))
                lo(area[:, bass.ds(at + O_LO, SEQ)], src, area[:, bass.ds(at + O_HI, SEQ)]).then_inc(o_set, 1)

            def used(k):
                dve.wait_ge(unit_done, c.next(unit_done))
                split(k)

            def rest_of_tile(t, layer, project):
                values_lo(0)
                turned_lo()
                if project:
                    stage(0, SCALE)
                else:
                    used(0)
                softmax(0, vec_done)
                output_lo(1, t - 1, layer)
                difference(layer)
                if project:
                    stage(1, 1.0)
                else:
                    used(1)
                turned_lo()

            def heads(t, layer, before):
                if before:
                    rest_of_tile(t, layer, project=True)
                    qk_lo(2, 0, 0)
                    qk_lo(2, 2, 1)
                else:
                    stage_qk(2, 2, 1)
                stage(2, 1.0)
                stick_softplus()
                if before:
                    output_lo(0, t - 1, layer)
                stage(3, SCALE)
                values_lo(2)
                stick_lo()
                stage(4, 1.0)
                qk_lo(1, 0, 3)
                stick_softplus()
                qk_lo(1, 2, 4)
                stage(5, 1.0)
                rows(t * 2, 0)
                stick_lo()
                stage(6, SCALE)
                softmax(0, prob_set)
                output_lo(2, t, layer)
                values_lo(1)
                rows(t * 2 + 1, 1)
                stage(7, 1.0)
                turned_lo()
                qk_lo(0, 0, 6)
                qk_lo(0, 2, 7)
                stage(8, 1.0)
                softmax(1, prob_set)
                rows(t + N_FOX, 0)

            def gates(splits=True):
                for k in range(3):
                    if splits:
                        dve.wait_ge(unit_done, c.next(unit_done))
                    elif k == 2:
                        dve.wait_ge(gate_out, c.peek(gate_out))
                    dve.tensor_tensor(tile(6 * (k % 2)), ps[:, k, :], rstd[:], ALU.mult).then_inc(tail_read, 1)
                    c.skip(tail_read)
                    if splits:
                        split(k)
                dve.wait_ge(gate_out, c.next(gate_out, 3))

            def mix(banks, at, inside):
                m, part = tile(4), tile(5)
                for b in range(3):
                    if b in inside:
                        dve.wait_ge(proj_mm, c.next(proj_mm))
                    elif inside == (0, 2):
                        dve.wait_ge(unit_done, c.next(unit_done))
                    dve.tensor_tensor(part if b else m, tile(1 + b), ps[:, banks[b], :], ALU.mult
                                      ).then_inc(tail_read, 1)
                    dve.wait_ge(tail_read, c.next(tail_read))
                    if b:
                        done = m_mid if b == 2 else vec_done
                        dve.tensor_tensor(m, m, part, ALU.add).then_inc(done, 1)
                        dve.wait_ge(done, c.next(done))
                    if b == 1 and inside == (0, 2):
                        split(0)
                dve.wait_ge(m_hi_set, c.next(m_hi_set))
                lo(area[:, bass.ds(at + M_LO, SEQ)], m, area[:, bass.ds(at + M_HI, SEQ)]).then_inc(m_set, 1)

            def mixer(layer, gain):
                forget(layer)
                heads(0, layer, False)
                with c.turns(1, NT) as t:
                    heads(t, layer, True)
                rest_of_tile(NT, layer, project=False)
                used(2)
                output_lo(0, NT - 1, layer)

                def pair(at):
                    mix((5, 6, 3), at, (0, 2))
                    used(1)
                    used(2)
                    gates()
                    mix((7, 4, 5), at + SEQ, (1,))

                gates(splits=False)
                with c.turns(0, ND // 2 - 1) as i:
                    pair(i * (2 * SEQ))
                    gates()
                pair((ND - 2) * SEQ)
                dve.memset(acc, 0.0).then_inc(vec_done, 1)
                dve.wait_ge(vec_done, c.next(vec_done))
                for d in range(ND):
                    dve.wait_ge(unit_done, c.next(unit_done))
                    update(d * SEQ, 6 + d % 2, 1.0, gain + d)
                    split(d % SLOTS)
                dve.wait_ge(unit_done, c.next(unit_done))
                split(2)

            dve.sem_inc(up_set, 3)
            dve.sem_inc(h_set, 2)
            dve.sem_inc(o_set, 1)
            dve.sem_inc(tail_read, 9)
            c.skip(up_set, 3)
            c.skip(h_set, 2)
            c.skip(tail_read, 9)
            dve.memset(acc, 0.0).then_inc(vec_done, 1)
            dve.wait_ge(vec_done, c.next(vec_done))
            for k in range(2):
                dve.wait_ge(x_landed[k], 16 * (3 - 2 * k))
                for d in range(k * ND // 2, (k + 1) * ND // 2):
                    u_part(d * SEQ, P_GAIN + d)
                    if d % (ND // 2) == 1:
                        split(k)
            for d in range(ND):
                add_square(first_square(d))
            split(2)
            dve.wait_ge(small_landed, 16 * 3)
            n = DEPTH * 2
            pairs = tile(4)[:, 0:n * HEAD]
            dve.tensor_tensor(pairs, SQ[:, 0:n * HEAD], SQ[:, n * HEAD:2 * n * HEAD], ALU.mult).then_inc(vec_done, 1)
            dve.wait_ge(vec_done, c.next(vec_done))
            dve.reduce_sum(lam[:, 8:8 + n], pairs.rearrange("p (a b) -> p a b", b=HEAD), AX_X).then_inc(lam_in, 1)
            dve.wait_ge(lam_out, 1)
            for layer in range(DEPTH):
                e = 4 + 2 * layer
                dve.tensor_tensor(lam[:, layer:layer + 1], lam[:, e + 1:e + 2], lam[:, e:e + 1], ALU.subtract).then_inc(vec_done, 1)
                dve.wait_ge(vec_done, c.next(vec_done))
                dve.tensor_scalar(lam[:, layer:layer + 1], lam[:, layer:layer + 1], -lam_init(layer), None,
                                  ALU.add).then_inc(vec_done, 1)
                dve.wait_ge(vec_done, c.next(vec_done))
                dve.tensor_scalar(lam[:, 2 + layer:3 + layer], par[:, P_SUBLN + layer:P_SUBLN + layer + 1],
                                  1.0 - lam_init(layer), None, ALU.mult).then_inc(vec_done, 1)
                dve.wait_ge(vec_done, c.next(vec_done))
            dve.tensor_copy(base_l[:], scratch[:, 1024:1024 + SEQ])
            dve.tensor_copy(base_r[:], scratch[:, 1024 + SEQ:1024 + 2 * SEQ]).then_inc(const_set, 1)
            with c.turns(0, DEPTH) as layer:
                ffn(layer * (3 * ND) + (P_GAIN + ND))
                mixer(layer, layer * (3 * ND) + (P_GAIN + 2 * ND))
                ffn(layer * (3 * ND) + (P_GAIN + 3 * ND))
            dve.wait_ge(rstd_set, c.next(rstd_set))
            for d in range(ND):
                g = P_GAIN + 3 * DEPTH * ND + d
                dve.scalar_tensor_tensor(tile(d), h[:, d * SEQ:(d + 1) * SEQ], par[:, g:g + 1], rstd[:],
                                         ALU.mult, ALU.mult).then_inc(y_set, 1)



def constants():
    k, q = np.arange(P)[:, None], np.arange(P)[None, :]
    c = np.zeros((P, C_END), np.float32)
    c[:, C_IDENT:C_IDENT + P] = k == q
    c[:, C_STRICT01:C_STRICT01 + P] = k < q
    c[:, C_ONES:C_ONES + P] = 1
    row, group = np.arange(P) % 32, np.arange(P) // 32
    for head in range(N_FOX):
        c[:, C_SEL + head] = row == head
    for head in range(N_DIFF):
        c[:, C_SEL + N_FOX + head] = (row == N_FOX) * 2.0 ** (-8.0 * (head + 1) / N_DIFF)
    for g, sign in enumerate((-1, -1, 1, 1)):
        c[:, C_MASK + g] = sign * ((group == g) & (row < N_FOX))
    c[:, C_EPS], c[:, C_EPS + 1] = EPS, SUBLN_EPS
    r = np.zeros((P, ROUNDED * P), np.float32)

    def block(n):
        return r[:, n * P:(n + 1) * P]

    block(R_IDENT)[:] = k == q
    block(R_CAUSAL)[:] = np.where(q > k, NEG, 0)
    block(R_STRICT)[:] = np.where(k >= q, NEG, 0)
    block(R_NEGTRI)[:] = np.where(k >= q, -1, 0)
    block(R_NEGONES)[:] = -1
    pos = np.arange(SEQ)
    b = np.zeros((P, 2 * SEQ), np.float32)
    left, right = b[:, :SEQ], b[:, SEQ:]
    left[(group >= 2) & (row < N_FOX)] = 1
    right[(group < 2) & (row < N_FOX)] = 1
    left[N_FOX], right[N_FOX] = -pos, 1
    left[2 * 32 + N_FOX], right[2 * 32 + N_FOX] = 1, pos
    return c, r, b


def weight_stream(a):
    empty = np.zeros((1, P, UNIT, P), np.float32)
    branch = {"a": 0, "b": 3 * 512, "c": 9 * 512 + N_FOX - 3 * 512}
    gate0 = 9 * 512 + N_FOX

    def columns(w, at, n=1):
        return w[:, at:at + n * P].reshape(ND, P, n, P).transpose(2, 1, 0, 3)

    def ffn(w1, w3, w2):
        both = np.stack([columns(w1, 0, NF), columns(w3, 0, NF)], 1).reshape(2 * NF, P, UNIT, P)
        down = w2.reshape(NF, P, ND, P).transpose(2, 1, 0, 3)
        down = np.concatenate([down, np.zeros((ND, P, W2_UNITS * UNIT - NF, P), np.float32)], 2)
        down = down.reshape(ND, P, W2_UNITS, UNIT, P).transpose(0, 2, 1, 3, 4).reshape(-1, P, UNIT, P)
        both = [both[:2], empty, both[2:]]
        return both + [down]

    parts = []
    for n in range(DEPTH):
        parts += ffn(a["ffn1_w1"][n], a["ffn1_w3"][n], a["ffn1_w2"][n])
        w_in = a["w_in"][n]
        for t in range(NT):
            for name in "cba":
                for which in range(3):
                    parts.append(columns(w_in, branch[name] + which * 512 + t * P))
        proj = np.concatenate([a[f"proj_{'abc'[b]}"][n].reshape(NT, P, ND, P) for b in TAIL_ORDER], 0)
        for d in range(0, ND, 2):
            gates = [[columns(w_in, gate0 + b * D_MODEL + e * P) for b in TAIL_ORDER] for e in (d, d + 1)]
            blocks = proj[:, :, d:d + 2].transpose(2, 0, 1, 3).reshape(3, UNIT, P, P).transpose(0, 2, 1, 3)
            parts += gates[0] + [blocks] + gates[1]
        parts += [columns(a["w_out"][n], 0, ND), empty]
        parts += ffn(a["ffn2_w1"][n], a["ffn2_w3"][n], a["ffn2_w2"][n])
    parts += [empty] * SLOTS
    return np.concatenate(parts, 0).reshape(-1, P, UNIT * P)


def small_params(a):
    p = np.zeros((P, P_END), np.float32)
    gains = []
    for n in range(DEPTH):
        gains += [a["ffn1_norm"][n], a["mix_norm"][n], a["ffn2_norm"][n]]
        p[:, P_SUBLN + n] = a["diff_subln"][n]
        p[:, P_FB + n] = np.tile(a["forget_bias"][n], P // N_FOX)
        wf = a["w_in"][n][:, 6 * 512:6 * 512 + N_FOX].reshape(ND, P, N_FOX).transpose(1, 0, 2)
        p[:, P_WF + n * ND * N_FOX:P_WF + (n + 1) * ND * N_FOX] = wf.reshape(P, -1)
    gains.append(a["final_norm"])
    p[:, P_GAIN:P_GAIN + GAINS * ND] = np.stack(gains).reshape(GAINS * ND, P).transpose(1, 0)
    return p


def lambda_rows(a):
    rows = [a[f"diff_l{x}{m}"][n] for x in "qk" for n in range(DEPTH) for m in (1, 2)]
    return np.tile(np.concatenate(rows)[None, :], (P, 1))


def kernel(**inputs):
    import concourse.bacc as bacc
    from concourse.bass_utils import run_bass_kernel_spmd

    a = {name: np.ascontiguousarray(v) for name, v in inputs.items()}
    c, r, b = constants()
    arrays = {
        "x": np.ascontiguousarray(a["x"][0].reshape(SEQ, ND, P).transpose(2, 1, 0)).reshape(P, ND * SEQ),
        "weights": weight_stream(a),
        "params": small_params(a),
        "lambdas": lambda_rows(a),
        "const": c, "const_r": r, "const_b": b,
    }
    nc = bacc.Bacc("TRN2", target_bir_lowering=False, num_devices=1, dynamic_dma_scratch_size=1024)
    aps = [nc.dram_tensor(name, v.shape, F32, kind="ExternalInput").ap() for name, v in arrays.items()]
    out = nc.dram_tensor("out", (P, ND * SEQ), F32, kind="ExternalOutput").ap()
    trunk(nc, *aps, out)
    got = run_bass_kernel_spmd(nc, [arrays], core_ids=[0]).results[0]["out"]
    return np.ascontiguousarray(got.reshape(P, ND, SEQ).transpose(2, 1, 0).reshape(1, SEQ, D_MODEL))
```
